# Optimizing a Trainium2 kernel written in Bass

```python
import math
import jax
import jax.numpy as jnp
from jax import lax
import numpy as np
import jax, jax.numpy as jnp

D_MODEL = 1024
BATCH = 1
SEQ = 256
DEPTH = 1

GRID_W = 64
CTX_LEN = 256
N_GROUPS = 4
GROUP_W = D_MODEL // N_GROUPS
GROUP_HEADS = 4
HEAD_DIM = GROUP_W // GROUP_HEADS
NA_WIN_H = 8
NA_WIN_W = 16
DN_CONV_K = 5
DN_CHUNK = 64
DIFF_DIM = HEAD_DIM // 2
Q_BLOCK = 128
FT_DIM = GROUP_W // GROUP_HEADS
N_EXPERTS = 16
EC_FACTOR = 2
D_EXPERT = 2 * D_MODEL
ROPE_BASE = 10000.0
RMS_EPS = 1e-6
IN_WIDTHS = (GROUP_W, GROUP_W, GROUP_W, 3 * GROUP_W, 2 * GROUP_HEADS, 2 * GROUP_HEADS, GROUP_W, GROUP_W, GROUP_W, GROUP_W, GROUP_W)
IN_W = 11 * GROUP_W + 4 * GROUP_HEADS
F32 = jnp.float32


def rmsnorm(x, g):
    xf = x.astype(F32)
    y = xf * lax.rsqrt(jnp.mean(xf * xf, axis=-1, keepdims=True) + RMS_EPS)
    return (y * g.astype(F32)).astype(x.dtype)

def l2norm(x):
    return x * lax.rsqrt(jnp.sum(x * x, axis=-1, keepdims=True) + 1e-6)

def modulate(h, shift, scale):
    return h * (1 + scale) + shift

def split_heads(t, d=HEAD_DIM):
    return t.reshape(*t.shape[:-1], t.shape[-1] // d, d)

def split_proj(p):
    idx, acc = [], 0
    for w in IN_WIDTHS[:-1]:
        acc += w
        idx.append(acc)
    return jnp.split(p, idx, axis=-1)

def axial_rope(n_tok, dim):
    t = jnp.arange(n_tok)
    pos = jnp.stack([t // GRID_W, t % GRID_W], axis=-1).astype(F32)
    n_freq = dim // 4
    inv = ROPE_BASE ** (-jnp.arange(n_freq, dtype=F32) / n_freq)
    ang = (pos[:, :, None] * inv).reshape(n_tok, 2 * n_freq)
    return jnp.cos(ang), jnp.sin(ang)

def apply_rope(x, cos, sin):
    xf = x.astype(F32).reshape(*x.shape[:-1], -1, 2)
    x1, x2 = xf[..., 0], xf[..., 1]
    out = jnp.stack([x1 * cos - x2 * sin, x1 * sin + x2 * cos], axis=-1)
    return out.reshape(x.shape).astype(x.dtype)

def softmax_attention(q, k, v):
    s = jnp.einsum('bqhd,bkhd->bhqk', q, k).astype(F32) * q.shape[-1] ** -0.5
    p = jax.nn.softmax(s, axis=-1)
    return jnp.einsum('bhqk,bkhd->bqhd', p, v.astype(F32))

def neighbourhood_attention(q, k, v, k_ctx, v_ctx, rpb):
    B, S, H, dh = q.shape
    rows = S // GRID_W
    wh = min(NA_WIN_H, rows)
    r = jnp.arange(rows)
    row_idx = jnp.clip(r - wh // 2, 0, rows - wh)[:, None] + jnp.arange(wh)[None, :]
    cq = jnp.arange(GRID_W)
    c0 = jnp.clip(cq - NA_WIN_W // 2, 0, GRID_W - NA_WIN_W)
    in_win = (cq[None, :] >= c0[:, None]) & (cq[None, :] < c0[:, None] + NA_WIN_W)
    dy = row_idx - r[:, None] + NA_WIN_H - 1
    dx = jnp.clip(cq[None, :] - cq[:, None], 1 - NA_WIN_W, NA_WIN_W - 1) + NA_WIN_W - 1
    bias = rpb[:, dy[:, None, :, None], dx[None, :, None, :]].astype(F32)
    qg = q.reshape(B, rows, GRID_W, H, dh)
    k_blk = k.reshape(B, rows, GRID_W, H, dh)[:, row_idx]
    v_blk = v.reshape(B, rows, GRID_W, H, dh)[:, row_idx]
    scale = dh ** -0.5
    s_win = jnp.einsum('brqhd,brwkhd->bhrqwk', qg, k_blk).astype(F32) * scale + bias
    s_win = jnp.where(in_win[:, None, :], s_win, -jnp.inf)
    s_ctx = jnp.einsum('brqhd,blhd->bhrql', qg, k_ctx).astype(F32) * scale
    n_win = wh * GRID_W
    p = jax.nn.softmax(jnp.concatenate([s_win.reshape(B, H, rows, GRID_W, n_win), s_ctx], axis=-1), axis=-1)
    p_win = p[..., :n_win].reshape(B, H, rows, GRID_W, wh, GRID_W)
    p_ctx = p[..., n_win:]
    out = jnp.einsum('bhrqwk,brwkhd->brqhd', p_win, v_blk.astype(F32)) + jnp.einsum('bhrql,blhd->brqhd', p_ctx, v_ctx.astype(F32))
    return out.reshape(B, S, H, dh)

def short_conv(u, w):
    return lax.conv_general_dilated(u, w[:, None, :].astype(u.dtype), window_strides=(1,), padding=[(DN_CONV_K // 2, DN_CONV_K // 2)], dimension_numbers=('NWC', 'WIO', 'NWC'), feature_group_count=u.shape[-1])

def chunk_gated_delta(q, k, v, g, beta, s0):
    B, T, H, dk = q.shape
    n, C = T // DN_CHUNK, DN_CHUNK

    def chunks(t):
        return jnp.swapaxes(t.reshape(B, n, C, H, *t.shape[3:]), 2, 3)
    qc, kc, vc, bc = chunks(q), chunks(k), chunks(v), chunks(beta)
    gc = jnp.cumsum(chunks(g), axis=-1)
    incl = jnp.tril(jnp.ones((C, C), bool))
    strict = jnp.tril(jnp.ones((C, C), bool), -1)
    decay = jnp.exp(jnp.where(incl, gc[..., :, None] - gc[..., None, :], -jnp.inf))
    kb = kc * bc[..., None]
    lower = jnp.where(strict, jnp.einsum('bnhid,bnhjd->bnhij', kb, kc) * decay, 0.0)
    eye = jnp.eye(C, dtype=F32)
    t_inv = lax.linalg.triangular_solve(eye + lower, jnp.broadcast_to(eye, lower.shape), left_side=True, lower=True, unit_diagonal=True)
    u = t_inv @ (vc * bc[..., None])
    w = t_inv @ (kb * jnp.exp(gc)[..., None])
    qk = jnp.where(incl, jnp.einsum('bnhid,bnhjd->bnhij', qc, kc) * decay, 0.0)
    q_dec = qc * jnp.exp(gc)[..., None]
    k_dec = kc * jnp.exp(gc[..., -1:] - gc)[..., None]
    g_last = jnp.exp(gc[..., -1])

    def step(s, xs):
        u_i, w_i, qk_i, qd_i, kd_i, gl_i = xs
        v_new = u_i - jnp.einsum('bhcd,bhde->bhce', w_i, s)
        o_i = jnp.einsum('bhcd,bhde->bhce', qd_i, s) + jnp.einsum('bhcj,bhje->bhce', qk_i, v_new)
        s = s * gl_i[..., None, None] + jnp.einsum('bhcd,bhce->bhde', kd_i, v_new)
        return s, o_i
    xs = tuple(jnp.swapaxes(t, 0, 1) for t in (u, w, qk, q_dec, k_dec, g_last))
    s_fin, o = lax.scan(step, s0, xs)
    o = jnp.swapaxes(jnp.swapaxes(o, 0, 1), 2, 3).reshape(B, T, H, -1)
    return o, s_fin

def gated_deltanet(lat, ctx, conv_w, a_log, dt_bias, norm_g):
    def prep(qkv, a, b):
        B, T, _ = qkv.shape
        qkv = jax.nn.silu(short_conv(qkv, conv_w)).astype(F32)
        q, k, v = [split_heads(t) for t in jnp.split(qkv, 3, axis=-1)]
        q = l2norm(q) * HEAD_DIM ** -0.5
        k = l2norm(k)
        a = a.astype(F32).reshape(B, T, 2, GROUP_HEADS)
        b = b.astype(F32).reshape(B, T, 2, GROUP_HEADS)
        g = -jnp.exp(a_log.astype(F32)) * jax.nn.softplus(a + dt_bias.astype(F32))
        return q, k, v, g, jax.nn.sigmoid(b)
    ql, kl, vl, gl, bl = prep(lat[0], lat[1], lat[2])
    qc, kc, vc, gc, bc = prep(ctx[0], ctx[1], ctx[2])
    s0 = jnp.zeros((ql.shape[0], GROUP_HEADS, HEAD_DIM, HEAD_DIM), F32)
    flip = lambda t: jnp.flip(t, axis=1)
    oc_f, sc_f = chunk_gated_delta(qc, kc, vc, gc[:, :, 0], bc[:, :, 0], s0)
    ol_f, _ = chunk_gated_delta(ql, kl, vl, gl[:, :, 0], bl[:, :, 0], sc_f)
    oc_b, sc_b = chunk_gated_delta(flip(qc), flip(kc), flip(vc), flip(gc[:, :, 1]), flip(bc[:, :, 1]), s0)
    ol_b, _ = chunk_gated_delta(flip(ql), flip(kl), flip(vl), flip(gl[:, :, 1]), flip(bl[:, :, 1]), sc_b)

    def finish(o, gate):
        y = rmsnorm(o, norm_g) * jax.nn.silu(split_heads(gate.astype(F32)))
        return y.reshape(gate.shape).astype(gate.dtype)
    return finish(ol_f + flip(ol_b), lat[3]), finish(oc_f + flip(oc_b), ctx[3])

def diff_core(q, k, v, lam):
    s = jnp.einsum('bqhmd,bkhmd->bhmqk', q, k).astype(F32) * q.shape[-1] ** -0.5
    p = jax.nn.softmax(s, axis=-1)
    a = p[:, :, 0] - lam * p[:, :, 1]
    return jnp.einsum('bhqk,bkhd->bqhd', a, v.astype(F32))

def fourier_mix(u, w):
    B, T, _ = u.shape
    uf = u.astype(F32).reshape(B, T, GROUP_HEADS, FT_DIM)
    y = jnp.fft.fft2(uf, axes=(1, 3), norm='ortho').real.reshape(B, T, GROUP_W)
    return (y @ w.astype(F32)).astype(u.dtype)

def expert_choice_ffn(h, w_router, w_gate, w_up, w_down):
    B, N, D = h.shape
    cap = EC_FACTOR * N // N_EXPERTS
    aff = jax.nn.softmax((h @ w_router).astype(F32), axis=-1)
    gate, idx = lax.top_k(jnp.swapaxes(aff, 1, 2), cap)
    xg = jax.vmap(lambda hb, ib: hb[ib])(h, idx)
    hid = jax.nn.silu(jnp.einsum('becd,edf->becf', xg, w_gate)) * jnp.einsum('becd,edf->becf', xg, w_up)
    y = jnp.einsum('becf,efd->becd', hid, w_down) * gate[..., None].astype(h.dtype)
    return jax.vmap(lambda yb, ib: jnp.zeros((N, D), yb.dtype).at[ib.reshape(-1)].add(yb.reshape(-1, D)))(y, idx)

def token_mixers(h_lat, h_ctx, w_in, rpb, conv_w, a_log, dt_bias, dn_g, df_lam, lam_init, df_g, ft_w, cos, sin, ctx_out):
    B, S, _ = h_lat.shape
    L = h_ctx.shape[1]
    (na_q, na_k, na_v, dn_qkv, dn_a, dn_b, dn_gate, df_q, df_k, df_v, ft_u) = split_proj(h_lat @ w_in)
    (cna_q, cna_k, cna_v, cdn_qkv, cdn_a, cdn_b, cdn_gate, cdf_q, cdf_k, cdf_v, cft_u) = split_proj(h_ctx @ w_in)
    diff_heads = lambda t: t.reshape(*t.shape[:-1], GROUP_HEADS, 2, DIFF_DIM)
    dt = h_lat.dtype
    o_na = neighbourhood_attention(split_heads(na_q), split_heads(na_k), split_heads(na_v), split_heads(cna_k), split_heads(cna_v), rpb)
    o_dn, c_dn = gated_deltanet((dn_qkv, dn_a, dn_b, dn_gate), (cdn_qkv, cdn_a, cdn_b, cdn_gate), conv_w, a_log, dt_bias, dn_g)
    lq1, lk1, lq2, lk2 = df_lam.astype(F32)
    lam = jnp.exp(jnp.sum(lq1 * lk1)) - jnp.exp(jnp.sum(lq2 * lk2)) + lam_init
    q_d = apply_rope(diff_heads(df_q), cos, sin)
    k_d = apply_rope(diff_heads(df_k), cos, sin)
    kc_d, vc_d = diff_heads(cdf_k), split_heads(cdf_v)
    k_all = jnp.concatenate([kc_d, k_d], axis=1)
    v_all = jnp.concatenate([vc_d, split_heads(df_v)], axis=1)
    q_blocks = jnp.swapaxes(q_d.reshape(B, S // Q_BLOCK, Q_BLOCK, GROUP_HEADS, 2, DIFF_DIM), 0, 1)
    o_df = lax.map(lambda qb: diff_core(qb, k_all, v_all, lam), q_blocks)
    o_df = jnp.swapaxes(o_df, 0, 1).reshape(B, S, GROUP_HEADS, HEAD_DIM)
    diff_out = lambda o: rmsnorm(o, df_g) * (1.0 - lam_init)
    o_ft = fourier_mix(ft_u, ft_w)
    mix_lat = jnp.concatenate([o_na.reshape(B, S, GROUP_W).astype(dt), o_dn.astype(dt), diff_out(o_df).reshape(B, S, GROUP_W).astype(dt), o_ft.astype(dt)], axis=-1)
    if not ctx_out:
        return mix_lat, None
    c_na = softmax_attention(split_heads(cna_q), split_heads(cna_k), split_heads(cna_v))
    c_df = diff_out(diff_core(diff_heads(cdf_q), kc_d, vc_d, lam))
    c_ft = fourier_mix(cft_u, ft_w)
    mix_ctx = jnp.concatenate([c_na.reshape(B, L, GROUP_W).astype(dt), c_dn.astype(dt), c_df.reshape(B, L, GROUP_W).astype(dt), c_ft.astype(dt)], axis=-1)
    return mix_lat, mix_ctx

def first_inputs(seed: int = 0) -> dict:
    key = jax.random.key(seed)
    ks = jax.random.split(key, 24)
    nrm = lambda k, shape, s: jax.random.normal(k, shape, F32) * s
    H = GROUP_HEADS
    a_init = jax.random.uniform(ks[9], (DEPTH, 2, H), F32, 1.0, 16.0)
    dt_init = jnp.exp(jax.random.uniform(ks[10], (DEPTH, 2, H), F32, math.log(1e-3), math.log(1e-1)))
    return {
        'x': nrm(ks[0], (BATCH, SEQ, D_MODEL), 1.0),
        'c': nrm(ks[1], (BATCH, D_MODEL), 1.0),
        'ctx': nrm(ks[2], (BATCH, CTX_LEN, D_MODEL), 1.0),
        'c_ctx': nrm(ks[3], (D_MODEL,), 1.0),
        'w_mod': nrm(ks[4], (DEPTH, D_MODEL, 6 * D_MODEL), 0.5 * D_MODEL ** -0.5),
        'b_mod': nrm(ks[5], (DEPTH, 6 * D_MODEL), 0.01),
        'norm1_g': 1.0 + nrm(ks[6], (DEPTH, D_MODEL), 0.02),
        'w_in': nrm(ks[7], (DEPTH, D_MODEL, IN_W), D_MODEL ** -0.5),
        'na_rpb': nrm(ks[8], (DEPTH, H, 2 * NA_WIN_H - 1, 2 * NA_WIN_W - 1), 0.02),
        'dn_conv_w': nrm(ks[11], (DEPTH, DN_CONV_K, 3 * GROUP_W), DN_CONV_K ** -0.5),
        'dn_a_log': jnp.log(a_init),
        'dn_dt_bias': dt_init + jnp.log(-jnp.expm1(-dt_init)),
        'dn_norm_g': 1.0 + nrm(ks[12], (DEPTH, HEAD_DIM), 0.02),
        'df_lambda': nrm(ks[13], (DEPTH, 4, DIFF_DIM), 0.1),
        'df_norm_g': 1.0 + nrm(ks[14], (DEPTH, HEAD_DIM), 0.02),
        'ft_w': nrm(ks[15], (DEPTH, GROUP_W, GROUP_W), GROUP_W ** -0.5),
        'w_out': nrm(ks[16], (DEPTH, D_MODEL, D_MODEL), D_MODEL ** -0.5),
        'norm2_g': 1.0 + nrm(ks[17], (DEPTH, D_MODEL), 0.02),
        'w_router': nrm(ks[18], (DEPTH, D_MODEL, N_EXPERTS), D_MODEL ** -0.5),
        'w_gate': nrm(ks[19], (DEPTH, N_EXPERTS, D_MODEL, D_EXPERT), D_MODEL ** -0.5),
        'w_up': nrm(ks[20], (DEPTH, N_EXPERTS, D_MODEL, D_EXPERT), D_MODEL ** -0.5),
        'w_down': nrm(ks[21], (DEPTH, N_EXPERTS, D_EXPERT, D_MODEL), D_EXPERT ** -0.5),
        'final_norm_g': 1.0 + nrm(ks[22], (D_MODEL,), 0.02),
    }

def first_block(x, c, ctx, c_ctx, w_mod, b_mod, norm1_g, w_in, na_rpb, dn_conv_w, dn_a_log, dn_dt_bias, dn_norm_g, df_lambda, df_norm_g, ft_w, w_out, norm2_g, w_router, w_gate, w_up, w_down, final_norm_g):
    S = x.shape[1]
    cos, sin = axial_rope(S, DIFF_DIM)
    cos, sin = cos[:, None, None, :], sin[:, None, None, :]
    s_lat = jax.nn.silu(c)
    s_ctx = jax.nn.silu(c_ctx)
    x_lat, x_ctx = x, ctx
    for l in range(DEPTH):
        ctx_out = l < DEPTH - 1
        lam_init = 0.8 - 0.6 * math.exp(-0.3 * l)
        m_lat = jnp.split((s_lat @ w_mod[l] + b_mod[l])[:, None, :], 6, axis=-1)
        m_ctx = jnp.split(s_ctx @ w_mod[l] + b_mod[l], 6, axis=-1)
        h_lat = modulate(rmsnorm(x_lat, norm1_g[l]), m_lat[0], m_lat[1])
        h_ctx = modulate(rmsnorm(x_ctx, norm1_g[l]), m_ctx[0], m_ctx[1])
        mix_lat, mix_ctx = token_mixers(h_lat, h_ctx, w_in[l], na_rpb[l], dn_conv_w[l], dn_a_log[l], dn_dt_bias[l], dn_norm_g[l], df_lambda[l], lam_init, df_norm_g[l], ft_w[l], cos, sin, ctx_out)
        x_lat = x_lat + m_lat[2] * (mix_lat @ w_out[l])
        h_lat = modulate(rmsnorm(x_lat, norm2_g[l]), m_lat[3], m_lat[4])
        x_lat = x_lat + m_lat[5] * expert_choice_ffn(h_lat, w_router[l], w_gate[l], w_up[l], w_down[l])
        if ctx_out:
            x_ctx = x_ctx + m_ctx[2] * (mix_ctx @ w_out[l])
            h_ctx = modulate(rmsnorm(x_ctx, norm2_g[l]), m_ctx[3], m_ctx[4])
            x_ctx = x_ctx + m_ctx[5] * expert_choice_ffn(h_ctx, w_router[l], w_gate[l], w_up[l], w_down[l])
    return rmsnorm(x_lat, final_norm_g)


D_RNN = 1280
RNN_BLOCKS = 10
RNN_BW = D_RNN // RNN_BLOCKS
CONV_W = 4
LRU_C = 8.0
N_HEADS = 8
HEAD_DIM_2 = 128
D_ATT = N_HEADS * HEAD_DIM_2
KV_RANK = 256
IDX_HEADS = 8
IDX_DIM = 64
TOPK_MAX = 256
IDX_SCALE = IDX_DIM ** -0.5 * IDX_HEADS ** -0.5
ATT_SCALE = HEAD_DIM_2 ** -0.5
EXP_PER_GROUP = 8
N_EXPERTS_2 = N_GROUPS * EXP_PER_GROUP
TOP_K_INNER = 2
D_EXPERT_2 = 512
MOE_BLOCK = 128
N_BRANCH = 2
EPS = 1e-6

SPLITS = (D_RNN, D_RNN, D_ATT, KV_RANK, IDX_HEADS * IDX_DIM, IDX_DIM, IDX_HEADS, N_BRANCH * D_MODEL)
D_IN = sum(SPLITS)


def rmsnorm_2(x, g):
    xf = x.astype(jnp.float32)
    y = xf * lax.rsqrt(jnp.mean(xf * xf, axis=-1, keepdims=True) + EPS)
    return (y * g.astype(jnp.float32)).astype(x.dtype)

def modulate_2(x, g, shift, scale):
    return rmsnorm_2(x, g) * (1 + scale[:, None, :]) + shift[:, None, :]

def causal_dwconv(x, w, b):
    y = lax.conv_general_dilated(x, w[:, None, :], window_strides=(1,), padding=[(CONV_W - 1, 0)],
                                 dimension_numbers=('NWC', 'WIO', 'NWC'), feature_group_count=x.shape[-1])
    return y + b

def rg_lru(x, w_a, b_a, w_x, b_x, lam):
    B_, S_, _ = x.shape
    xb = x.reshape(B_, S_, RNN_BLOCKS, RNN_BW)
    r = jax.nn.sigmoid(jnp.einsum('bsnc,ncd->bsnd', xb, w_a).reshape(B_, S_, D_RNN) + b_a)
    i = jax.nn.sigmoid(jnp.einsum('bsnc,ncd->bsnd', xb, w_x).reshape(B_, S_, D_RNN) + b_x)
    log_a = -LRU_C * jax.nn.softplus(-lam.astype(jnp.float32)) * r.astype(jnp.float32)
    a = jnp.exp(log_a)
    inp = jnp.sqrt(-jnp.expm1(2.0 * log_a)) * (i * x).astype(jnp.float32)

    def combine(lhs, rhs):
        a1, b1 = lhs
        a2, b2 = rhs
        return a1 * a2, a2 * b1 + b2

    _, h = lax.associative_scan(combine, (a, inp), axis=1)
    return h.astype(x.dtype)

def dsa_attention(q, c_kv, q_idx, k_idx, w_idx, w_uk, w_uv):
    B_, S_ = q.shape[0], q.shape[1]
    topk = min(TOPK_MAX, S_ // 4)
    nblk = S_ // Q_BLOCK
    slopes = 2.0 ** (-8.0 * jnp.arange(1, N_HEADS + 1, dtype=jnp.float32) / N_HEADS)
    key_pos = jnp.arange(S_)

    def to_blocks(t):
        return jnp.moveaxis(t.reshape((B_, nblk, Q_BLOCK) + t.shape[2:]), 1, 0)

    def one_block(args):
        qb, qib, wib, q0 = args
        qpos = q0 + jnp.arange(Q_BLOCK)
        causal = key_pos[None, :] <= qpos[:, None]
        rel = jax.nn.relu(jnp.einsum('bqhd,bsd->bqhs', qib, k_idx).astype(jnp.float32))
        score = jnp.einsum('bqh,bqhs->bqs', wib.astype(jnp.float32), rel) * IDX_SCALE
        score = jnp.where(causal[None], score, -jnp.inf)
        _, sel = lax.top_k(score, topk)
        c_sel = jax.vmap(lambda cb, ib: cb[ib])(c_kv, sel)
        q_lat = jnp.einsum('bqhd,rhd->bqhr', qb, w_uk)
        logits = jnp.einsum('bqhr,bqkr->bqhk', q_lat, c_sel).astype(jnp.float32) * ATT_SCALE
        dist = (qpos[None, :, None] - sel).astype(jnp.float32)
        logits = logits - slopes[None, None, :, None] * dist[:, :, None, :]
        valid = sel <= qpos[None, :, None]
        logits = jnp.where(valid[:, :, None, :], logits, -jnp.inf)
        p = jax.nn.softmax(logits, axis=-1).astype(c_sel.dtype)
        o_lat = jnp.einsum('bqhk,bqkr->bqhr', p, c_sel)
        return jnp.einsum('bqhr,rhd->bqhd', o_lat, w_uv)

    out = lax.map(one_block, (to_blocks(q), to_blocks(q_idx), to_blocks(w_idx), jnp.arange(nblk) * Q_BLOCK))
    return jnp.moveaxis(out, 0, 1).reshape(B_, S_, N_HEADS * HEAD_DIM_2)

def hier_moe(x, w_group, b_group, w_expert, b_expert, w1, w3, w2):
    B_, S_, D_ = x.shape
    T = B_ * S_
    xf = x.reshape(T, D_)
    g_logits = (xf @ w_group + b_group).astype(jnp.float32)
    g_sel = jnp.argmax(g_logits, axis=-1)
    g_w = jnp.take_along_axis(jax.nn.softmax(g_logits, axis=-1), g_sel[:, None], axis=-1)
    e_logits = (xf @ w_expert + b_expert).astype(jnp.float32).reshape(T, N_GROUPS, EXP_PER_GROUP)
    e_logits = jnp.take_along_axis(e_logits, g_sel[:, None, None], axis=1)[:, 0]
    e_top, e_loc = lax.top_k(e_logits, TOP_K_INNER)
    gate = (g_w * jax.nn.softmax(e_top, axis=-1)).reshape(-1)
    eid = (g_sel[:, None] * EXP_PER_GROUP + e_loc).reshape(-1)
    tok = jnp.repeat(jnp.arange(T, dtype=jnp.int32), TOP_K_INNER)
    A = T * TOP_K_INNER
    order = jnp.argsort(eid)
    eid_s = eid[order]
    counts = jnp.bincount(eid, length=N_EXPERTS_2)
    padded = (counts + MOE_BLOCK - 1) // MOE_BLOCK * MOE_BLOCK
    start = jnp.cumsum(counts) - counts
    pstart = jnp.cumsum(padded) - padded
    dest = pstart[eid_s] + jnp.arange(A) - start[eid_s]
    n_rows = A + N_EXPERTS_2 * MOE_BLOCK
    n_blk = n_rows // MOE_BLOCK
    row_tok = jnp.zeros((n_rows,), jnp.int32).at[dest].set(tok[order])
    row_gate = jnp.zeros((n_rows,), x.dtype).at[dest].set(gate[order].astype(x.dtype))
    blk_exp = jnp.minimum(jnp.searchsorted(jnp.cumsum(padded), jnp.arange(n_blk) * MOE_BLOCK, side='right'),
                          N_EXPERTS_2 - 1)
    xs = xf[row_tok].reshape(n_blk, MOE_BLOCK, D_)

    def expert_block(args):
        xb, e = args
        hid = jax.nn.silu(xb @ w1[e]) * (xb @ w3[e])
        return hid @ w2[e]

    ys = lax.map(expert_block, (xs, blk_exp)).reshape(n_rows, D_)
    out = jax.ops.segment_sum(ys * row_gate[:, None], row_tok, num_segments=T)
    return out.reshape(B_, S_, D_)

def _w(k, shape, fan_in, mult=1.0):
    return jax.random.normal(k, shape, jnp.float32) * (mult * fan_in ** -0.5)

def _small(k, shape):
    return 0.01 * jax.random.normal(k, shape, jnp.float32)

def _gain(k, shape):
    return 1.0 + 0.01 * jax.random.normal(k, shape, jnp.float32)

def second_inputs(seed: int = 0) -> dict:
    key = jax.random.key(seed)
    ks = list(jax.random.split(key, 32))
    L = DEPTH
    u = jax.random.uniform(ks.pop(), (L, D_RNN), jnp.float32, minval=0.9, maxval=0.999)
    a0 = u ** (1.0 / LRU_C)
    lru_lambda = jnp.log(a0) - jnp.log1p(-a0)
    return {
        'x': jax.random.normal(ks.pop(), (BATCH, SEQ, D_MODEL), jnp.float32),
        'c': jax.random.normal(ks.pop(), (BATCH, D_MODEL), jnp.float32),
        'w_mod': _w(ks.pop(), (L, D_MODEL, 6 * D_MODEL), D_MODEL, 0.5),
        'b_mod': _small(ks.pop(), (L, 6 * D_MODEL)),
        'norm1_g': _gain(ks.pop(), (L, D_MODEL)),
        'w_in': _w(ks.pop(), (L, D_MODEL, D_IN), D_MODEL),
        'conv_w': _w(ks.pop(), (L, CONV_W, D_RNN), CONV_W),
        'conv_b': _small(ks.pop(), (L, D_RNN)),
        'w_rg_a': _w(ks.pop(), (L, RNN_BLOCKS, RNN_BW, RNN_BW), RNN_BW),
        'b_rg_a': _small(ks.pop(), (L, D_RNN)),
        'w_rg_x': _w(ks.pop(), (L, RNN_BLOCKS, RNN_BW, RNN_BW), RNN_BW),
        'b_rg_x': _small(ks.pop(), (L, D_RNN)),
        'lru_lambda': lru_lambda,
        'kv_norm_g': _gain(ks.pop(), (L, KV_RANK)),
        'w_uk': _w(ks.pop(), (L, KV_RANK, N_HEADS, HEAD_DIM_2), KV_RANK),
        'w_uv': _w(ks.pop(), (L, KV_RANK, N_HEADS, HEAD_DIM_2), KV_RANK),
        'w_rnn_out': _w(ks.pop(), (L, D_RNN, D_MODEL), D_RNN),
        'w_att_out': _w(ks.pop(), (L, D_ATT, D_MODEL), D_ATT),
        'w_out': _w(ks.pop(), (L, D_MODEL, D_MODEL), D_MODEL),
        'norm2_g': _gain(ks.pop(), (L, D_MODEL)),
        'w_group': _w(ks.pop(), (L, D_MODEL, N_GROUPS), D_MODEL),
        'b_group': _small(ks.pop(), (L, N_GROUPS)),
        'w_expert': _w(ks.pop(), (L, D_MODEL, N_EXPERTS_2), D_MODEL),
        'b_expert': _small(ks.pop(), (L, N_EXPERTS_2)),
        'moe_w1': _w(ks.pop(), (L, N_EXPERTS_2, D_MODEL, D_EXPERT_2), D_MODEL),
        'moe_w3': _w(ks.pop(), (L, N_EXPERTS_2, D_MODEL, D_EXPERT_2), D_MODEL),
        'moe_w2': _w(ks.pop(), (L, N_EXPERTS_2, D_EXPERT_2, D_MODEL), D_EXPERT_2),
        'final_g': _gain(ks.pop(), (D_MODEL,)),
    }

def second_block(x, c, w_mod, b_mod, norm1_g, w_in, conv_w, conv_b, w_rg_a, b_rg_a, w_rg_x, b_rg_x,
              lru_lambda, kv_norm_g, w_uk, w_uv, w_rnn_out, w_att_out, w_out, norm2_g, w_group, b_group,
              w_expert, b_expert, moe_w1, moe_w3, moe_w2, final_g):
    B_, S_, _ = x.shape
    split_pts = [int(v) for v in np.cumsum(SPLITS)[:-1]]
    h = x
    for l in range(DEPTH):
        mod = jax.nn.silu(c) @ w_mod[l] + b_mod[l]
        sh1, sc1, g1, sh2, sc2, g2 = jnp.split(mod, 6, axis=-1)
        u = modulate_2(h, norm1_g[l], sh1, sc1)
        proj = u @ w_in[l]
        xr, gr, q, ckv, qi, ki, wi, mg = jnp.split(proj, split_pts, axis=-1)
        hr = rg_lru(causal_dwconv(xr, conv_w[l], conv_b[l]), w_rg_a[l], b_rg_a[l], w_rg_x[l], b_rg_x[l],
                    lru_lambda[l])
        y_a = (jax.nn.gelu(gr) * hr) @ w_rnn_out[l]
        att = dsa_attention(q.reshape(B_, S_, N_HEADS, HEAD_DIM_2), rmsnorm_2(ckv, kv_norm_g[l]),
                            qi.reshape(B_, S_, IDX_HEADS, IDX_DIM), ki, wi, w_uk[l], w_uv[l])
        y_b = att @ w_att_out[l]
        ga, gb = jnp.split(jax.nn.sigmoid(mg), N_BRANCH, axis=-1)
        mix = (ga * y_a + gb * y_b) @ w_out[l]
        h = h + g1[:, None, :] * mix
        u2 = modulate_2(h, norm2_g[l], sh2, sc2)
        h = h + g2[:, None, :] * hier_moe(u2, w_group[l], b_group[l], w_expert[l], b_expert[l],
                                          moe_w1[l], moe_w3[l], moe_w2[l])
    return rmsnorm_2(h, final_g)


def setup_inputs(seed=0):
    out = dict(first_inputs(seed))
    for name, value in second_inputs(seed + 1).items():
        if name != "x":
            out[name + "_2"] = value
    return out


def reference(
    x, c, ctx, c_ctx, w_mod, b_mod, norm1_g, w_in, na_rpb, dn_conv_w, dn_a_log, dn_dt_bias,
    dn_norm_g, df_lambda, df_norm_g, ft_w, w_out, norm2_g, w_router, w_gate, w_up, w_down,
    final_norm_g, c_2, w_mod_2, b_mod_2, norm1_g_2, w_in_2, conv_w_2, conv_b_2, w_rg_a_2,
    b_rg_a_2, w_rg_x_2, b_rg_x_2, lru_lambda_2, kv_norm_g_2, w_uk_2, w_uv_2, w_rnn_out_2,
    w_att_out_2, w_out_2, norm2_g_2, w_group_2, b_group_2, w_expert_2, b_expert_2, moe_w1_2,
    moe_w3_2, moe_w2_2, final_g_2,
):
    x = first_block(
        x, c, ctx, c_ctx, w_mod, b_mod, norm1_g, w_in, na_rpb, dn_conv_w, dn_a_log, dn_dt_bias,
        dn_norm_g, df_lambda, df_norm_g, ft_w, w_out, norm2_g, w_router, w_gate, w_up, w_down,
        final_norm_g,
    )
    return second_block(
        x, c_2, w_mod_2, b_mod_2, norm1_g_2, w_in_2, conv_w_2, conv_b_2, w_rg_a_2, b_rg_a_2,
        w_rg_x_2, b_rg_x_2, lru_lambda_2, kv_norm_g_2, w_uk_2, w_uv_2, w_rnn_out_2, w_att_out_2,
        w_out_2, norm2_g_2, w_group_2, b_group_2, w_expert_2, b_expert_2, moe_w1_2, moe_w3_2,
        moe_w2_2, final_g_2,
    )


_drawn_inputs = setup_inputs


def setup_inputs(seed=0):
    import zlib

    import numpy as np

    out = dict(_drawn_inputs(seed))
    spreads = {}
    factors = {'b_mod': 3.514,
     'norm1_g': 5.575,
     'na_rpb': 8.0,
     'dn_norm_g': 7.57,
     'df_norm_g': 7.905,
     'norm2_g': 5.543,
     'b_mod_2': 3.404,
     'norm1_g_2': 5.158,
     'conv_b_2': 8.0,
     'b_rg_a_2': 8.0,
     'b_rg_x_2': 8.0,
     'kv_norm_g_2': 8.0,
     'norm2_g_2': 7.917,
     'b_group_2': 8.0,
     'b_expert_2': 8.0,
     'final_g_2': 5.77}
    for name, (base, spread) in spreads.items():
        noise = np.random.default_rng([zlib.crc32(name.encode()), seed]).standard_normal(out[name].shape)
        drawn = base * np.exp(spread * noise) if base else spread * noise
        out[name] = jnp.asarray(drawn.astype(out[name].dtype))
    for name, factor in factors.items():
        out[name] = (out[name] * factor).astype(out[name].dtype)
    return out
```

```python
import numpy as np
import concourse.bass as bass
from concourse import mybir
from contextlib import ExitStack

F32 = mybir.dt.float32
I32 = mybir.dt.int32
ACT = mybir.ActivationFunctionType
ALU = mybir.AluOpType
AX = mybir.AxisListType

P = 128
D = 1024
KT = D // P
S = 256
NT = S // P
GW = 256
H = 4
HD = 64
GRID = 64
CONV = 5
E1, F1 = 16, 2048
CAP1 = 2 * S // E1
E2, F2 = 32, 512
CAP2 = 64
PASSES2 = S // CAP2
NG2, EPG2 = 4, 8
DR = 1280
RT = DR // P
CONV2 = 4
AH = 8
AD = 128
KVR = 256
IH, IDD = 8, 64
TOPK = S // 4
EPS = 1e-6
NEG = -1e30
LAM_INIT = 0.8 - 0.6 * float(np.exp(-0.3 * 0))
WORDS = 2048
SLOTS = 12
FRONT = 4
LEVELS = [1, 2, 4, 8, 16, 32, 64]
IDX_SCALE = IDD ** -0.5 * IH ** -0.5
ATT_SCALE = AD ** -0.5

W_IN = dict(dn_k=1024, dn_v=1280, dn_q=768, na_q=0, na_k=256, df_q=1808, df_k=2064, na_v=512, df_v=2320,
            dn_gate=1552, ft_u=2576)
BOTH = ("dn_k", "dn_v", "na_k", "df_k")
W_IN_AB = 1536

IN2 = [3584, 3840, 4096, 2560, 2816, 3072, 3328] + [256 * i for i in range(10)] + [4424 + 256 * i for i in range(8)]
IN2_KI, IN2_WI = 4352, 4416


class Layout:

    def __init__(self, **widths):
        self.at, n = {}, 0
        for name, w in widths.items():
            self.at[name] = (n, n + w)
            n += w
        self.width = n

    def of(self, view, name):
        a, b = self.at[name]
        return view[:, a:b]


CONST1 = Layout(ident=P, ones=P, tri_f=P, tri_b=P, strict_f=P, strict_b=P, level_f=7 * P, level_b=7 * P,
                window=GRID, rope_r=P, cos=S, sin=S, dft=2 * 512, bd_cos=P, bd_sin=P, pick=2, slot=CAP2)
CONST2 = Layout(neg_dist=NT * S, causal=NT * S, group_no=NG2, expert_no=E2)
SMALL = Layout(norm1=KT, norm1_2=KT, c=KT, c_ctx=KT, c_2=KT, conv=6 * CONV, a_log=8, dt_bias=8, dn_norm=HD,
               df_norm=HD, df_lambda=128, router_b=NG2 + E2, conv_2=RT * CONV2, conv_b_2=RT, rg_a=RT, rg_x=RT,
               lru=RT, kv_norm=KVR)


def const_arrays():
    i = np.arange(P)
    r, c = i[:, None], i[None, :]
    t = {}
    t["ident"] = r == c
    t["ones"] = np.ones((P, P))
    t["tri_f"], t["tri_b"] = r <= c, r >= c
    t["strict_f"], t["strict_b"] = c < r, c > r
    lv = [(r // (2 * b) == c // (2 * b)) & ((r // b) % 2 == 1) & ((c // b) % 2 == 0) for b in LEVELS]
    t["level_f"] = np.concatenate(lv, axis=1)
    t["level_b"] = np.concatenate([m.T for m in lv], axis=1)
    q, k = (i % GRID)[:, None], np.arange(GRID)[None, :]
    c0 = np.clip(q - 8, 0, GRID - 16)
    t["window"] = np.where((k >= c0) & (k < c0 + 16), 0.0, NEG)
    rr = np.zeros((P, P))
    ev = np.arange(0, P, 2)
    rr[ev + 1, ev] = -1.0
    rr[ev, ev + 1] = 1.0
    t["rope_r"] = rr
    tok = np.arange(S)
    inv = np.float32(10000.0) ** (-np.arange(8, dtype=np.float32) / np.float32(8))
    pos = np.stack([tok // GRID, tok % GRID], -1).astype(np.float32)
    ang = (pos[:, :, None] * inv.astype(np.float32)).reshape(S, 16).astype(np.float64)
    pair = (i % 32) // 2
    t["cos"], t["sin"] = np.cos(ang)[:, pair].T, np.sin(ang)[:, pair].T
    w = 2 * np.pi * np.outer(tok, tok) % (2 * np.pi * S) / S
    dft = np.concatenate([np.cos(w), np.sin(w)], axis=1)
    t["dft"] = dft.reshape(NT, P, 512).transpose(1, 0, 2).reshape(P, 1024)
    w = 2 * np.pi * ((i[:, None] % HD) * (i[None, :] % HD) % HD) / HD
    same = (r // HD) == (c // HD)
    t["bd_cos"], t["bd_sin"] = np.cos(w) * same / 128, -np.sin(w) * same / 128
    t["pick"] = np.stack([i % 32 == 0, i % 32 == 1], 1)
    t["slot"] = np.broadcast_to(np.arange(CAP2), (P, CAP2))
    u = {}
    qp = (np.arange(NT)[None, :, None] * P + i[:, None, None])
    u["neg_dist"] = (tok[None, None, :] - qp).reshape(P, -1)
    u["causal"] = np.where(tok[None, None, :] <= qp, 0.0, NEG).reshape(P, -1)
    u["group_no"] = np.broadcast_to(np.arange(NG2), (P, NG2))
    u["expert_no"] = np.broadcast_to(np.arange(E2) // EPG2, (P, E2))
    pack = lambda lay, tab: np.ascontiguousarray(
        np.concatenate([np.asarray(tab[n], np.float32) for n in lay.at], axis=1))
    return pack(CONST1, t), pack(CONST2, u)


class Banks:

    def __init__(self, psum, filled, emptied):
        self.psum, self.filled, self.emptied, self.order = psum, filled, emptied, {}

    def new(self, key):
        self.order[key] = len(self.order)
        return self.tile(key)

    def tile(self, key):
        return self.psum[:, self.order[key] % 8, :]

    def when_full(self, key):
        return self.filled[self.order[key] % 8]

    def when_read(self, key):
        return self.emptied[self.order[key] % 8]

    def free(self, key):
        n = self.order[key]
        return self.emptied[n % 8], n // 8 + 1

    def full(self, key):
        n = self.order[key]
        return self.filled[n % 8], n // 8 + 1

    def read_out(self, key):
        n = self.order[key]
        return self.emptied[n % 8], n // 8 + 2

    def last(self, b):
        return self.emptied[b], max(i for i in self.order.values() if i % 8 == b) // 8 + 2


def build(nc, A, out):
    ctx = ExitStack()
    with ctx:
        def sem(name):
            return ctx.enter_context(nc.semaphore(name))

        pe_step = sem("pe_step")
        act_step = sem("act_step")
        dve_step = sem("dve_step")
        pool_step = sem("pool_step")
        m_onehot = sem("m_onehot")
        m_xg = sem("m_xg")
        m_gathered = sem("m_gathered")
        m_hid = sem("m_hid")
        m_chunk_used = sem("m_chunk_used")
        m_hidT = sem("m_hidT")
        m_turned = sem("m_turned")
        m_y = sem("m_y")
        m_acc = sem("m_acc")
        m_spread = sem("m_spread")
        m_silu = sem("m_silu")
        n_onehot = sem("n_onehot")
        n_xg = sem("n_xg")
        n_rows = sem("n_rows")
        n_rows_turned = sem("n_rows_turned")
        n_gathered = sem("n_gathered")
        n_hid = sem("n_hid")
        n_chunk_used = sem("n_chunk_used")
        n_y = sem("n_y")
        n_acc = sem("n_acc")
        n_spread = sem("n_spread")
        n_hidT = sem("n_hidT")
        n_turned = sem("n_turned")
        n_silu = sem("n_silu")
        const2_loaded = sem("const2_loaded")
        xn2_ready = sem("xn2_ready")
        ckv_normed = sem("ckv_normed")
        xc_ready = sem("xc_ready")
        prob2_ready = sem("prob2_ready")
        gh_ready = sem("gh_ready")
        mix2_ready = sem("mix2_ready")
        u2_ready = sem("u2_ready")
        wrt2_loaded = sem("wrt2_loaded")
        masks_ready = sem("masks_ready")
        flag_ready = sem("flag_ready")
        diag_ready = sem("diag_ready")
        consts_loaded = sem("consts_loaded")
        xn_ready = sem("xn_ready")
        svec_ready = sem("svec_ready")
        bmod_loaded = sem("bmod_loaded")
        ftw_loaded = sem("ftw_loaded")
        h_ready = sem("h_ready")
        wab_loaded = sem("wab_loaded")
        conv_silu = sem("conv_silu")
        g_ready = sem("g_ready")
        kq_normed = sem("kq_normed")
        na_bias_ready = sem("na_bias_ready")
        roped = sem("roped")
        prob_ready = sem("prob_ready")
        lower_ready = sem("lower_ready")
        inverse_begun = sem("inverse_begun")
        vk_ready = sem("vk_ready")
        kd_ready = sem("kd_ready")
        qk_ready = sem("qk_ready")
        mix_ready = sem("mix_ready")
        h2_ready = sem("h2_ready")
        wrt_loaded = sem("wrt_loaded")
        aff_ready = sem("aff_ready")
        choice_ready = sem("choice_ready")
        mixers_done = sem("mixers_done")
        block1_ready = sem("block1_ready")
        mixers2_done = sem("mixers2_done")
        out_ready = sem("out_ready")
        stored = sem("stored")
        x_loaded = sem("x_loaded")
        ctx_loaded = sem("ctx_loaded")
        small_loaded = sem("small_loaded")
        svec_zero = sem("svec_zero")
        squares_ready = sem("squares_ready")
        pad_zero = sem("pad_zero")
        conv_ready = sem("conv_ready")
        na_bias_loaded = sem("na_bias_loaded")
        softplus_arg = sem("softplus_arg")
        softplus_exp = sem("softplus_exp")
        smax_ready = sem("smax_ready")
        prob_exp = sem("prob_exp")
        decay_arg = sem("decay_arg")
        decay_exp = sem("decay_exp")
        gls_ready = sem("gls_ready")
        gain_loaded = sem("gain_loaded")
        x1_ready = sem("x1_ready")
        rt_max = sem("rt_max")
        rt_exp = sem("rt_exp")
        x2_ready = sem("x2_ready")
        lru_arg = sem("lru_arg")
        lru_exp = sem("lru_exp")
        relu_used = sem("relu_used")
        xr_zero = sem("xr_zero")
        rg_ready = sem("rg_ready")
        la_ready = sem("la_ready")
        decay2_ready = sem("decay2_ready")
        lru_var = sem("lru_var")
        lru_std = sem("lru_std")
        smax2_ready = sem("smax2_ready")
        exp2_ready = sem("exp2_ready")
        mg_ready = sem("mg_ready")
        gain2_loaded = sem("gain2_loaded")
        x3_ready = sem("x3_ready")
        group_max = sem("group_max")
        route_exp = sem("route_exp")
        x4_ready = sem("x4_ready")
        half_ready = sem("half_ready")
        rstd_ready = sem("rstd_ready")
        kq_squares = sem("kq_squares")
        kq_rstd = sem("kq_rstd")
        begc_ready = sem("begc_ready")
        decay_masked = sem("decay_masked")
        head_squares = sem("head_squares")
        head_rstd = sem("head_rstd")
        chosen_ready = sem("chosen_ready")
        hbias_ready = sem("hbias_ready")
        hbias_used = sem("hbias_used")
        pass_begun = sem("pass_begun")
        state_ready = [sem(f"state{d}_ready") for d in range(2)]
        vnew_ready = [sem(f"vnew{d}_ready") for d in range(2)]

        MAIN = 28300
        ring = ctx.enter_context(nc.sbuf_tensor("ring", [P, SLOTS * WORDS], F32))
        main = ctx.enter_context(nc.sbuf_tensor("main", [P, MAIN], F32))
        psum = ctx.enter_context(nc.psum_tensor("psum", [P, 8, 512], F32))
        cursor = {"main": 0, "late": FRONT * WORDS}

        def take(n, where="main"):
            a = cursor[where]
            cursor[where] = a + n
            assert a + n <= (MAIN if where == "main" else SLOTS * WORDS), (where, a + n)
            return (main if where == "main" else ring)[:, a:a + n]

        def slot(i):
            return ring[:, i * WORDS:(i + 1) * WORDS]

        banks = Banks(psum, [sem(f"bank{b}_filled") for b in range(8)], [sem(f"bank{b}_emptied") for b in range(8)])
        loaded = [sem(f"slot{s}_loaded") for s in range(SLOTS)]

        stream1 = [("w_mod", c) for c in range(8)] + [("w_in", c) for c in range(11)] + \
                  [("w_mod", c) for c in range(8, 24)] + [("w_mod_2", c) for c in range(24)] + \
                  [("w_out", c) for c in range(4)]
        stream2 = [("w_in_2", c) for c in range(3)] + [("w_ki", 0)] + [("w_in_2", c) for c in range(3, 7)] + \
                  [("w_uk", 0), ("w_uv", 0)] + [("w_in_2", c) for c in range(7, 17)] + [("w_rg", c) for c in range(2)] + \
                  [("w_in_2", c) for c in range(17, 25)] + [("w_rnn_out", c) for c in range(8)] + \
                  [("w_att_out", c) for c in range(4)] + [("w_out_2", c) for c in range(4)]
        loads = [0] * SLOTS
        placed, holder = {}, [None] * SLOTS
        plan1, plan2 = [], []
        for plan, stream in ((plan1, stream1), (plan2, stream2)):
            for n, key in enumerate(stream):
                s = n % FRONT
                plan.append((key, s, holder[s]))
                loads[s] += 1
                holder[s] = key
                placed[key] = (s, 16 * loads[s])
            if plan is plan1:
                base1, holder1 = list(loads), list(holder)
                loads = [v + E1 * 24 // SLOTS for v in loads]
                holder = [None] * SLOTS
            else:
                base2, holder2 = list(loads), list(holder)
        last_user = {}

        def arrived(key):
            return loaded[placed[key][0]], placed[key][1]

        def chunk(key):
            return slot(placed[key][0])

        cst = take(CONST1.width)
        K = lambda name: CONST1.of(cst, name)
        ident, ones = K("ident"), K("ones")
        sml = take(SMALL.width)
        M = lambda name: SMALL.of(sml, name)
        x = take(NT * D).rearrange("p (t d) -> p t d", t=NT)
        mfm = take(2 * 48 * 2).rearrange("p (b k m) -> p b k m", b=2, m=2)
        half = take(1)
        block_start = dict(cursor)

        h3 = take(KT * 2 * S).rearrange("p (k t) -> p k t", k=KT)
        hT = h3.rearrange("p k t -> p (k t)")
        cx = take(NT * D)
        ctx_in = cx.rearrange("p (t d) -> p t d", t=NT)
        bmod = take(2 * 256)
        svec = take(2 * KT * 32).rearrange("p (b k m) -> p b k m", b=2, k=KT)
        mpart = take(2 * 512).rearrange("p (i n) -> p i n", i=2)
        scale_fm = take(2 * KT).rearrange("p (m k) -> p m k", m=2)
        stat = take(64)
        padf = take(10 * 260)
        pad_kv = padf[:, 0:8 * 260].rearrange("p (c s n) -> p c s n", c=4, s=2)
        pad_q = padf[:, 8 * 260:].rearrange("p (c n) -> p c n", c=2)
        conv = take(5 * 512)
        conv_kv = conv[:, 0:2048].rearrange("p (c s t) -> p c s t", c=4, s=2)
        conv_q = conv[:, 2048:2560].rearrange("p (c t) -> p c t", c=2)
        na_q = take(2 * S).rearrange("p (f t) -> p f t", f=2)
        df_q = take(2 * S).rearrange("p (f t) -> p f t", f=2)
        v_tm = take(4 * 512).rearrange("p (t n) -> p t n", t=4)
        gate_tm = take(2 * GW).rearrange("p (t n) -> p t n", t=2)
        ft_u = take(2 * GW).rearrange("p (t n) -> p t n", t=2)
        ab = take(64).rearrange("p (t n) -> p t n", t=4)
        w_ab = take(KT * 16).rearrange("p (k n) -> p k n", k=KT)
        sp = take(6 * 32).rearrange("p (i n) -> p i n", i=6)
        g_log = take(32).rearrange("p (t d h) -> p t d h", t=4, d=2)
        beta = take(32).rearrange("p (t d h) -> p t d h", t=4, d=2)
        gcum = take(32).rearrange("p (d t h) -> p d t h", d=2, t=4)
        egc = take(32).rearrange("p (d t h) -> p d t h", d=2, t=4)
        begc = take(32).rearrange("p (d t h) -> p d t h", d=2, t=4)
        glast = take(32).rearrange("p (d t h) -> p d t h", d=2, t=4)
        ekd = take(32).rearrange("p (d t h) -> p d t h", d=2, t=4)
        gls = take(16).rearrange("p (d t h) -> p d t h", d=2, t=4)
        nlam = take(8)
        smax = take(64).rearrange("p (i n) -> p i n", i=4)
        ft_o = take(2 * S).rearrange("p (k t) -> p k t", k=2)
        mixf = take(NT * 768)
        mix = mixf.rearrange("p (t n) -> p t n", t=NT)
        ft_w = mixf[:, 0:512].rearrange("p (k n) -> p k n", k=2)
        ft_wc = mixf[:, 512:1536].rearrange("p (k i n) -> p k i n", k=2, i=2)
        kv_tm = padf[:, 0:2048].rearrange("p (t n) -> p t n", t=4)
        q_tm = padf[:, 2048:2560].rearrange("p (t n) -> p t n", t=2)
        kqT = conv[:, 0:2048].rearrange("p (t c n) -> p t c n", t=4, c=4)
        vk = conv[:, 2048:2560].rearrange("p (i h n) -> p i h n", i=2, h=H)
        solve = [hT[:, 2048 * d:2048 * d + 2048].rearrange("p (i h n) -> p i h n", i=4, h=H) for d in range(2)]
        c4 = cx.rearrange("p (i h n) -> p i h n", i=4, h=H)
        kk_sb, dmat, emat, etm = c4[:, 0], c4[:, 1], c4[:, 2], c4[:, 3]
        ft_a = cx[:, 0:1024].rearrange("p (f n) -> p f n", f=2)
        scratch = cx[:, 1024:2048]
        mixT = hT[:, 0:6 * S].rearrange("p (k t) -> p k t", k=6)
        xn = take(4 * D, "late").rearrange("p (t d) -> p t d", t=4)
        cursor["late"] -= 4 * D
        uw = take(8 * 512, "late").rearrange("p (d t n) -> p d t n", d=2, t=4)
        kd = take(8 * GW, "late").rearrange("p (d t h n) -> p d t h n", d=2, t=4, h=H)
        qk = take(4 * 512, "late").rearrange("p (d t h n) -> p d t h n", d=2, t=2, h=H)
        na_bias = take(8 * S, "late").rearrange("p (i n) -> p i n", i=8)
        prob = take(3 * 512, "late").rearrange("p (i n) -> p i n", i=3)
        pT = take(2 * 512, "late").rearrange("p (i c q) -> p i c q", i=2, c=4)
        na_k = take(4 * S, "late").rearrange("p (f t) -> p f t", f=2)
        df_k = take(4 * S, "late").rearrange("p (f t) -> p f t", f=2)
        o_acc = take(NT * GW, "late").rearrange("p (t h n) -> p t h n", t=NT, h=H)
        state = take(2 * 128, "late").rearrange("p (d g n) -> p d g n", d=2, g=2)
        vnew = take(2 * GW, "late").rearrange("p (d h n) -> p d h n", d=2, h=H)
        front1_end = dict(cursor)

        cursor.update(block_start)
        moe = take(KT * 2 * S)
        rows = take(3 * D).rearrange("p (i d) -> p i d", i=3)
        diag = take(512).rearrange("p (c n) -> p c n", c=4)
        h2 = take(NT * D).rearrange("p (t d) -> p t d", t=NT)
        h2T = take(KT * S).rearrange("p (k t) -> p k t", k=KT)
        acc = take(NT * D).rearrange("p (t d) -> p t d", t=NT)
        w_rt = take(KT * E1).rearrange("p (k e) -> p k e", k=KT)
        rt = take(NT * E1).rearrange("p (t e) -> p t e", t=NT)
        aff = take(5 * S).rearrange("p (i t) -> p i t", i=5)
        top8 = take(8)
        pg_tm = take(64).rearrange("p (i t e) -> p i t e", i=2, t=NT)
        rstat = take(16)
        assert cursor["main"] <= front1_end["main"] - 768 * 2 - 512
        onehot = moe[:, 0:128].rearrange("p (t s) -> p t s", t=NT)
        gated = moe[:, 128:384].rearrange("p (t s) -> p t s", t=NT)
        sgate, hid, hidT, ysb = (moe[:, 896 + 512 * i:1408 + 512 * i] for i in range(4))
        spread = moe[:, 2944:3200]
        xg1 = moe[:, 384:640].rearrange("p (k s) -> p k s", k=KT)

        PAIRS = [(0, p) for p in range(4, 12)] + [(1, p) for p in range(12)]
        ATT = [("na", h, t) for h in range(H) for t in range(NT)] + [("df", h, t) for h in range(H) for t in range(NT)]
        NA_N = len(ATT)
        CHUNKS = list(W_IN)
        TILES_OF = dict(na_v=range(4), df_v=range(4), dn_gate=(2, 3), ft_u=(2, 3))
        GROUPS = [(t, d) for t in range(4) for d in range(2)]
        ORDER = [(step, d, (0, 1, 2, 3)[step] if d == 0 else (1, 0, 3, 2)[step]) for step in range(4) for d in range(2)]
        G = lambda t, d: 2 * t + d
        FILL_LEVELS = (1, 3, 5)
        ROWS = ["gate1", "scale2", "shift2", "gate2", "b_gate1", "b_scale2", "b_shift2", "b_gate2"]
        ROW_OF = {"gate1": 2, "scale2": 4, "shift2": 3, "gate2": 5}
        BANK_G, BANK_U, BANK_T, BANK_Y, BANK_X, BANK_P, BANK_S = range(7)

        def moe1_tensor(pe, e):
            mm = nc.tensor.matmul
            pe.wait_ge(m_onehot, e + 1)
            pe.wait_ge(m_xg, e + 1)
            o = psum[:, BANK_X, :]
            for k in range(KT):
                for t in range(NT):
                    mm(o[:, CAP1 * k:CAP1 * k + CAP1], h2[:, t, P * k:P * k + P], onehot[:, t, 0:CAP1], start=t == 0, stop=t == NT - 1)
            for t in range(NT):
                last = mm(psum[:, BANK_P, P * t:P * t + P], gated[:, t, :], ident, start=True, stop=True)
            last.then_inc(m_gathered, 1)
            pe.wait_ge(m_xg, e + 2)
            pe.wait_ge(m_hid, e + 1)
            for k in range(KT):
                for i, b in enumerate((BANK_G, BANK_U)):
                    n = 2 * k + i
                    pe.wait_ge(loaded[n % SLOTS], 32 * e + 16 * (base1[n % SLOTS] + n // SLOTS + 1))
                    for j in range(4):
                        last = mm(psum[32 * j:32 * j + 32, b, :], xg1[:, k, :], slot(n % SLOTS)[:, 512 * j:512 * j + 512],
                                  start=k == 0, stop=k == KT - 1)
                    last.then_inc(m_chunk_used, 1)
            pe.wait_ge(m_hid, e + 2)
            pe.wait_ge(m_hidT, e + 1)
            for c in range(4):
                last = nc.tensor.transpose(psum[:, BANK_T, P * c:P * c + P], hid[:, P * c:P * c + P], ident)
            last.then_inc(m_turned, 1)
            pe.wait_ge(m_hidT, e + 2)
            pe.wait_ge(m_y, e + 1)
            for n in range(16, 24):
                w = slot(n % SLOTS).rearrange("p (r n) -> p r n", r=2)
                pe.wait_ge(loaded[n % SLOTS], 32 * e + 16 * (base1[n % SLOTS] + n // SLOTS + 1))
                for r in range(2):
                    f = 2 * (n - 16) + r
                    for g in range(2):
                        q = 32 * (2 * g + r)
                        last = mm(psum[q:q + 32, BANK_Y, :], hidT[:, P * (f % 4) + 32 * (f // 4):P * (f % 4) + 32 * (f // 4) + 32],
                                  w[:, r, 512 * g:512 * g + 512], start=n == 16, stop=n == 23)
                last.then_inc(m_chunk_used, 1)
            pe.wait_ge(m_y, e + 2)
            for t in range(NT):
                pe.wait_ge(m_acc, 2 * e + t + 1)
                for g in range(2):
                    last = mm(psum[:, BANK_S + g, :], spread[64 * g:64 * g + 64, P * t:P * t + P], ysb[64 * g:64 * g + 64, :],
                              start=True, stop=True)
                last.then_inc(m_spread, 1)

        def counter():
            n = [0]

            def count():
                n[0] += 1
                return n[0]
            return count

        pe_steps, act_steps, dve_steps, pool_steps = (counter() for _ in range(4))

        def hpart(h):
            return slice(64 * (h % 2), 64 * (h % 2) + 64)

        def moe1_vector(dve, e):
            V = nc.vector
            dve.wait_ge(m_gathered, e + 1)
            for t in range(NT):
                pos = pg_tm[:, 0, t, bass.ds(e, 1)]
                V.tensor_scalar(onehot[:, t, 0:CAP1], K("slot")[:, 0:CAP1], pos, None, ALU.is_equal)
                last = V.tensor_scalar(gated[:, t, :].rearrange("p (g s) -> p g s", g=4),
                                       K("slot")[:, 0:CAP1].unsqueeze(1).to_broadcast([P, 4, CAP1]),
                                       pos, pg_tm[:, 1, t, bass.ds(e, 1)], ALU.is_equal, ALU.mult)
            last.then_inc(m_onehot, 1)
            dve.wait_ge(m_silu, e + 1)
            dve.wait_ge(m_turned, e + 1)
            V.tensor_tensor(hid, sgate, psum[:, BANK_U, :], ALU.mult).then_inc(m_hid, 1)
            for t in range(NT):
                dve.wait_ge(m_spread, 2 * e + t + 2)
                dve.wait_ge(m_acc, 2 * e + t + 1)
                V.tensor_tensor(acc[:, t, :], acc[:, t, :], psum[:, BANK_S:BANK_S + 2, :].rearrange("p b n -> p (b n)"),
                                ALU.add).then_inc(m_acc, 1)

        def moe1_scalar(act, e):
            act.wait_ge(m_gathered, e + 2)
            act.wait_ge(m_spread, 2 * e + 1)
            act.activation(xg1.rearrange("p k s -> p (k s)"), psum[:, BANK_X, 0:KT * CAP1], ACT.Copy)
            act.activation(spread, psum[:, BANK_P, 0:S], ACT.Copy).then_inc(m_xg, 1)
            act.wait_ge(m_chunk_used, 24 * e + 16)
            act.wait_ge(m_hid, e + 1)
            act.activation(sgate, psum[:, BANK_G, :], ACT.Silu).then_inc(m_silu, 1)
            act.wait_ge(m_turned, e + 2)
            act.activation(hidT, psum[:, BANK_T, :], ACT.Copy).then_inc(m_hidT, 1)
            act.wait_ge(m_chunk_used, 24 * e + 24)
            act.activation(ysb, psum[:, BANK_Y, :], ACT.Copy).then_inc(m_y, 1)

        def moe1_load(sp, e, n):
            s = n % SLOTS
            name, c = (("w_gate", "w_up")[n % 2], n // 2) if n < 16 else ("w_down", n - 16)
            src = A[name][8 * e + c] if isinstance(e, int) else \
                A[name][bass.ds(8 * e + c, 1), :, :].rearrange("e p n -> p (e n)")
            sp.dma_start(slot(s), src).then_inc(loaded[s], 16)

        def log1p(V, dve, y, s, s2, q):
            V.tensor_scalar(s, y, 2.0, None, ALU.add).then_inc(dve_step, 1)
            dve.wait_ge(dve_step, dve_steps())
            V.reciprocal(s, s).then_inc(dve_step, 1)
            dve.wait_ge(dve_step, dve_steps())
            V.tensor_tensor(s, s, y, ALU.mult).then_inc(dve_step, 1)
            dve.wait_ge(dve_step, dve_steps())
            V.tensor_tensor(s2, s, s, ALU.mult).then_inc(dve_step, 1)
            dve.wait_ge(dve_step, dve_steps())
            V.tensor_scalar(q, s2, 1.0 / 17, None, ALU.mult).then_inc(dve_step, 1)
            dve.wait_ge(dve_step, dve_steps())
            for n in (15, 13, 11, 9, 7, 5, 3):
                V.scalar_tensor_tensor(q, q, 1.0 / n, s2, ALU.add, ALU.mult).then_inc(dve_step, 1)
                dve.wait_ge(dve_step, dve_steps())
            V.scalar_tensor_tensor(q, q, 1.0, s, ALU.add, ALU.mult).then_inc(dve_step, 1)
            dve.wait_ge(dve_step, dve_steps())
            V.tensor_scalar(q, q, 2.0, None, ALU.mult).then_inc(dve_step, 1)
            dve.wait_ge(dve_step, dve_steps())

        cursor.update(block_start)
        c2 = take(CONST2.width)
        K2 = lambda name: CONST2.of(c2, name)
        small2 = take(256)
        cl, nsp = small2[:, 0:RT], small2[:, 16:16 + 5 * RT].rearrange("p (i n) -> p i n", i=5)
        stat2 = small2[:, 72:112]
        wi = small2[:, 112:128].rearrange("p (t h) -> p t h", t=NT)
        scale2 = small2[:, 128:136]
        smax2 = small2[:, 136:168].rearrange("p (i t) -> p i t", t=NT)
        top2 = small2[:, 168:184].rearrange("p (t n) -> p t n", t=NT)
        relu = take(512).rearrange("p (i n) -> p i n", i=2)
        gr = take(RT * S).rearrange("p (c t) -> p c t", c=RT)
        moe2_start = cursor["main"]
        uT = take(KT * S).rearrange("p (k t) -> p k t", k=KT)
        LEAD = CONV2 - 1
        xr = take(RT * (S + LEAD)).rearrange("p (c t) -> p c t", c=RT)
        xc = take(RT * S).rearrange("p (c t) -> p c t", c=RT)
        rb = take(RT * S).rearrange("p (c t) -> p c t", c=RT)
        la = take(RT * S).rearrange("p (c t) -> p c t", c=RT)
        th = take(RT * S).rearrange("p (c t) -> p c t", c=RT)
        cursor["late"] = FRONT * WORDS
        q2f = take(AH * S, "late")
        q2 = q2f.rearrange("p (h t) -> p h t", h=AH)
        xn2 = q2f.rearrange("p (t d) -> p t d", t=NT)
        qif = take(4 * S, "late")
        qi = qif.rearrange("p (c t) -> p c t", c=4)
        pT2 = qif.rearrange("p (i s q) -> p i s q", i=2, s=NT)
        ki = take(S, "late")
        ckvf = take(NT * KVR, "late")
        ckv = ckvf.rearrange("p (t r) -> p t r", t=NT)
        ckvT = take(2 * S, "late").rearrange("p (r t) -> p r t", r=2)
        k2f = take(AH * S, "late")
        k2 = k2f.rearrange("p (h t) -> p h t", h=AH)
        mixT2 = k2f.rearrange("p (k t) -> p k t", k=KT)
        v2 = take(NT * D, "late").rearrange("p (t n) -> p t n", t=NT)
        attT = take(AH * S, "late").rearrange("p (h t) -> p h t", h=AH)
        mg = take(16 * S, "late").rearrange("p (c t) -> p c t", c=16)
        swf = take(1024, "late")
        score, work2 = (swf[:, 512 * i:512 * i + 512].rearrange("p (t s) -> p t s", t=NT) for i in range(2))
        prob2 = swf.rearrange("p (i t s) -> p i t s", i=2, t=NT)
        chosen = take(512, "late")
        hbias = [relu.rearrange("p i n -> p (i n)"), ckvf]
        cursor["main"] = moe2_start
        rows2 = take(3 * D).rearrange("p (i d) -> p i d", i=3)
        diag2 = take(512).rearrange("p (c n) -> p c n", c=4)
        u2 = take(NT * D).rearrange("p (t d) -> p t d", t=NT)
        u2T = take(KT * S).rearrange("p (k t) -> p k t", k=KT)
        acc2 = take(NT * D).rearrange("p (t d) -> p t d", t=NT)
        w_rt2 = take(KT * (NG2 + E2)).rearrange("p (k e) -> p k e", k=KT)
        lg = take(NT * (NG2 + E2)).rearrange("p (t e) -> p t e", t=NT)
        rt2 = take(8 * 64).rearrange("p (i t e) -> p i t e", i=8, t=NT)
        idx8 = take(16).bitcast(mybir.dt.uint32).rearrange("p (t n) -> p t n", t=NT)
        top8b = take(16).rearrange("p (t n) -> p t n", t=NT)
        rs2 = take(64)
        flag = take(1).bitcast(I32)
        onehot2 = take(NT * CAP2).rearrange("p (t s) -> p t s", t=NT)
        gated2 = take(NT * P).rearrange("p (t s) -> p t s", t=NT)
        xg2 = take(KT * CAP2).rearrange("p (k g s) -> p k g s", k=4, g=2)
        xrow2 = take(512)
        sg2, hid2, hidT2 = take(256), take(256), take(256)
        y2 = take(512)
        spread2 = take(2 * S).rearrange("p (i t) -> p i t", i=2)
        masks, gates2, pos2 = rt2[:, 0], rt2[:, 1], rt2[:, 2]

        IDXB = [(t, par, pr) for t in range(NT) for par in range(2) for pr in range(2)]
        SLOPES = [2.0 ** (-8.0 * (h + 1) / AH) for h in range(AH)]
        KIND2 = ["ckv"] + ["qi"] * 2 + ["q"] * 4 + ["xr"] * 5 + ["gr"] * 5 + ["mg"] * 8
        FIRST2 = {k: KIND2.index(k) for k in KIND2}

        def moe2_load(sp, j, n):
            u, c = n // 6, n % 6
            name, h = (("moe_w1", "moe_w3")[c % 2], c // 2) if c < 4 else ("moe_w2", c - 4)
            src = A[name][2 * (2 * j + u) + h] if isinstance(j, int) else \
                A[name][bass.ds(4 * j + (2 * u + h), 1), :, :].rearrange("e p n -> p (e n)")
            sp.dma_start(slot(n), src).then_inc(loaded[n], 16)


        def gather2(pe, i):
            pe.wait_ge(n_onehot, i + 1)
            pe.wait_ge(n_xg, i + 1)
            for t in range(NT):
                for g in range(2):
                    nc.tensor.matmul(psum[64 * g:64 * g + 64, BANK_X, :], onehot2[:, t, :], u2[:, t, 512 * g:512 * g + 512],
                                     start=t == 0, stop=t == NT - 1)
            for t in range(NT):
                last = nc.tensor.matmul(psum[:, BANK_P, P * t:P * t + P], gated2[:, t, :], ident, start=True, stop=True)
            last.then_inc(n_gathered, 1)

        def turn_tokens2(pe, i):
            pe.wait_ge(n_rows, i + 1)
            for c in range(4):
                last = nc.tensor.transpose(psum[:, BANK_X, P * c:P * c + P], xrow2[:, P * c:P * c + P], ident)
            last.then_inc(n_rows_turned, 1)

        def up2(pe, i, j, u):
            pe.wait_ge(n_xg, i + 2)
            pe.wait_ge(n_hid, i + 1)
            for c in range(4):
                n = 6 * u + c
                b = (BANK_G, BANK_U)[c % 2]
                w = slot(n).rearrange("p (k n) -> p k n", k=4)
                pe.wait_ge(loaded[n], 16 * j + 16 * (base2[n] + 1))
                for k in range(4):
                    for q in range(2):
                        last = nc.tensor.matmul(psum[64 * q:64 * q + 64, b, 0:256], xg2[:, k, c // 2, :], w[:, k, 256 * q:256 * q + 256],
                                                start=c < 2 and k == 0, stop=c >= 2 and k == 3)
                last.then_inc(n_chunk_used, 1)

        def spread_out2(pe, i, u, t):
            pe.wait_ge(n_y, i + 2)
            pe.wait_ge(n_acc, 2 * i + t + 1)
            for g in range(2):
                last = nc.tensor.matmul(psum[:, BANK_S + g, :], spread2[64 * g:64 * g + 64, u, P * t:P * t + P],
                                        y2[64 * g:64 * g + 64, :], start=True, stop=True)
            last.then_inc(n_spread, 1)

        def turn2(pe, i):
            pe.wait_ge(n_hid, i + 2)
            pe.wait_ge(n_hidT, i + 1)
            for c in range(2):
                last = nc.tensor.transpose(psum[:, BANK_T, P * c:P * c + P], hid2[:, P * c:P * c + P], ident)
            last.then_inc(n_turned, 1)

        def down2(pe, i, j, u):
            pe.wait_ge(n_hidT, i + 2)
            pe.wait_ge(n_y, i + 1)
            for q in range(2):
                n = 6 * u + 4 + q
                w = slot(n).rearrange("p (r n) -> p r n", r=2)
                pe.wait_ge(loaded[n], 16 * j + 16 * (base2[n] + 1))
                for c in range(2):
                    for g in range(2):
                        last = nc.tensor.matmul(psum[64 * g:64 * g + 64, BANK_Y, :], hidT2[:, P * c + CAP2 * q:P * c + CAP2 * q + CAP2],
                                                w[:, c, 512 * g:512 * g + 512], start=q == 0 and c == 0, stop=q == 1 and c == 1)
                last.then_inc(n_chunk_used, 1)

        def pair2_tensor(pe, j, first=False, final=False):
            for u in range(2):
                i = 2 * j + u
                up2(pe, i, j, u)
                if not (first and u == 0):
                    spread_out2(pe, i - 1, 1 - u, 0)
                turn2(pe, i)
                if not (final and u == 1):
                    gather2(pe, i + 1)
                if not (first and u == 0):
                    spread_out2(pe, i - 1, 1 - u, 1)
                if not (final and u == 1):
                    turn_tokens2(pe, i + 1)
                down2(pe, i, j, u)

        def onehot_2(dve, i, e):
            dve.wait_ge(n_gathered, i + 1)
            for t in range(NT):
                pos = pos2[:, t, e:e + 1] if isinstance(e, int) else pos2[:, t, bass.ds(e, 1)]
                gate = gates2[:, t, e:e + 1] if isinstance(e, int) else gates2[:, t, bass.ds(e, 1)]
                nc.vector.tensor_scalar(onehot2[:, t, :], K("slot"), pos, None, ALU.is_equal)
                last = nc.vector.tensor_scalar(gated2[:, t, :].rearrange("p (g s) -> p g s", g=2),
                                               K("slot").unsqueeze(1).to_broadcast([P, 2, CAP2]), pos, gate, ALU.is_equal, ALU.mult)
            last.then_inc(n_onehot, 1)

        def hidden2(dve, i):
            dve.wait_ge(n_silu, i + 1)
            dve.wait_ge(n_turned, i + 1)
            nc.vector.tensor_tensor(hid2, sg2, psum[:, BANK_U, 0:256], ALU.mult).then_inc(n_hid, 1)

        def add2(dve, i):
            for t in range(NT):
                dve.wait_ge(n_spread, 2 * i + t + 2)
                dve.wait_ge(n_acc, 2 * i + t + 1)
                nc.vector.tensor_tensor(acc2[:, t, :], acc2[:, t, :], psum[:, BANK_S:BANK_S + 2, :].rearrange("p b n -> p (b n)"),
                                        ALU.add).then_inc(n_acc, 1)

        def pair2_vector(dve, p, jj, first=False, final=False):
            for u in range(2):
                i, e = 32 * p + 2 * jj + u, 2 * jj + u
                if not (final and u == 1):
                    onehot_2(dve, i + 1, e + 1)
                hidden2(dve, i)
                if not (first and u == 0):
                    add2(dve, i - 1)

        def read_gathered2(act, i, u, spread_done=None):
            act.wait_ge(n_gathered, i + 2)
            nc.scalar.activation(xrow2, psum[:, BANK_X, :], ACT.Copy).then_inc(n_rows, 1)
            if spread_done is not None:
                act.wait_ge(n_spread, spread_done)
            nc.scalar.activation(spread2[:, u, :], psum[:, BANK_P, 0:S], ACT.Copy)
            act.wait_ge(n_rows_turned, i + 1)
            nc.scalar.activation(xg2.rearrange("p k g s -> p (k g s)"), psum[:, BANK_X, :], ACT.Copy).then_inc(n_xg, 1)

        def pair2_scalar(act, j, first=False, final=False):
            for u in range(2):
                i = 2 * j + u
                act.wait_ge(n_chunk_used, 6 * i + 4)
                act.wait_ge(n_hid, i + 1)
                nc.scalar.activation(sg2, psum[:, BANK_G, 0:256], ACT.Silu).then_inc(n_silu, 1)
                act.wait_ge(n_turned, i + 2)
                nc.scalar.activation(hidT2, psum[:, BANK_T, 0:256], ACT.Copy).then_inc(n_hidT, 1)
                if not (final and u == 1):
                    read_gathered2(act, i + 1, 1 - u, None if first and u == 0 else 2 * i + 1)
                else:
                    act.wait_ge(n_spread, 2 * i + 1)
                act.wait_ge(n_chunk_used, 6 * i + 6)
                nc.scalar.activation(y2, psum[:, BANK_Y, :], ACT.Copy).then_inc(n_y, 1)

        def block2_tensor(pe, flip, row_out):
            mm = nc.tensor.matmul
            pe.wait_ge(m_acc, 2 * E1 + 1)
            pe.wait_ge(const2_loaded, 16)
            for kk in range(4):
                o = banks.new(("uT", kk))
                pe.wait_ge(*banks.free(("uT", kk)))
                pe.wait_ge(xn2_ready, NT)
                for c in range(2):
                    for t in range(NT):
                        last = flip(o[:, S * c + P * t:S * c + P * t + P], xn2[:, t, P * (2 * kk + c):P * (2 * kk + c) + P])
                last.then_inc(banks.when_full(("uT", kk)), 1)
            for kk in range(4):
                pe.wait_ge(*banks.read_out(("uT", kk)))

            def project(ci):
                pe.wait_ge(*arrived(("w_in_2", ci)))
                w = chunk(("w_in_2", ci)).rearrange("p (k n) -> p k n", k=KT)
                o = banks.new(("in2", ci))
                pe.wait_ge(*banks.free(("in2", ci)))
                for f in range(2):
                    for k in range(KT):
                        if KIND2[ci] == "ckv":
                            last = mm(o[:, 256 * f:256 * f + 256], uT[:, k, P * f:P * f + P], w[:, k, :], start=k == 0, stop=k == KT - 1)
                        else:
                            last = mm(o[:, 256 * f:256 * f + 256], w[:, k, P * f:P * f + P], uT[:, k, :], start=k == 0, stop=k == KT - 1)
                last.then_inc(banks.when_full(("in2", ci)), 1)
                last_user[("w_in_2", ci)] = ("in2", ci)

            for ci in range(3):
                project(ci)
            pe.wait_ge(*arrived(("w_ki", 0)))
            w = chunk(("w_ki", 0))[:, 0:KT * (2 * IDD + IH)].rearrange("p (k n) -> p k n", k=KT)
            o = banks.new("ki")
            pe.wait_ge(*banks.free("ki"))
            for k in range(KT):
                mm(o[:, 0:S], w[:, k, 0:P], uT[:, k, :], start=k == 0, stop=k == KT - 1)
            for t in range(NT):
                for k in range(KT):
                    last = mm(o[:, S + IH * t:S + IH * t + IH], uT[:, k, P * t:P * t + P], w[:, k, P:P + IH], start=k == 0, stop=k == KT - 1)
            last.then_inc(banks.when_full("ki"), 1)
            last_user[("w_ki", 0)] = "ki"
            for ci in (1, 2):
                pe.wait_ge(*banks.read_out(("in2", ci)))
            pe.wait_ge(*banks.read_out("ki"))
            for t, par, pr in IDXB:
                o = banks.new(("idx", t, par, pr))
                pe.wait_ge(*banks.free(("idx", t, par, pr)))
                for m in range(2):
                    h = 4 * pr + 2 * m + par
                    last = mm(o[:, S * m:S * m + S], qi[hpart(h), h // 2, P * t:P * t + P], ki[hpart(h), :], start=True, stop=True)
                last.then_inc(banks.when_full(("idx", t, par, pr)), 1)
            o = banks.new("ckvT")
            pe.wait_ge(*banks.free("ckvT"))
            pe.wait_ge(ckv_normed, 1)
            for r in range(2):
                for t in range(NT):
                    last = flip(o[:, S * r + P * t:S * r + P * t + P], ckv[:, t, P * r:P * r + P])
            last.then_inc(banks.when_full("ckvT"), 1)
            for ci in range(3, 7):
                project(ci)
            pe.wait_ge(*banks.read_out("ckvT"))
            pe.wait_ge(*arrived(("w_uk", 0)))
            w = chunk(("w_uk", 0)).rearrange("p (r n) -> p r n", r=2)
            for hh in range(AH // 2):
                o = banks.new(("k2", hh))
                pe.wait_ge(*banks.free(("k2", hh)))
                for m in range(2):
                    h = 2 * hh + m
                    for r in range(2):
                        last = mm(o[:, S * m:S * m + S], w[:, r, AD * h:AD * h + AD], ckvT[:, r, :], start=r == 0, stop=r == 1)
                last.then_inc(banks.when_full(("k2", hh)), 1)
            last_user[("w_uk", 0)] = ("k2", 3)
            pe.wait_ge(*arrived(("w_uv", 0)))
            w = chunk(("w_uv", 0)).rearrange("p (r n) -> p r n", r=2)
            for t in range(NT):
                for g in range(2):
                    o = banks.new(("v2", t, g))
                    pe.wait_ge(*banks.free(("v2", t, g)))
                    for r in range(2):
                        last = mm(o[:, :], ckvT[:, r, P * t:P * t + P], w[:, r, 512 * g:512 * g + 512], start=r == 0, stop=r == 1)
                    last.then_inc(banks.when_full(("v2", t, g)), 1)
            last_user[("w_uv", 0)] = ("v2", 1, 1)
            for ci in range(7, 17):
                project(ci)
            for g in range(2):
                pe.wait_ge(*arrived(("w_rg", g)))
                w = chunk(("w_rg", g))[:, 0:RT // 2 * 2 * P].rearrange("p (n i c) -> p n i c", n=RT // 2, i=2)
                for m in range(RT // 2):
                    n = RT // 2 * g + m
                    o = banks.new(("rg", n))
                    pe.wait_ge(*banks.free(("rg", n)))
                    pe.wait_ge(xc_ready, n + 1)
                    for i in range(2):
                        last = mm(o[:, S * i:S * i + S], w[:, m, i, :], xc[:, n, :], start=True, stop=True)
                    last.then_inc(banks.when_full(("rg", n)), 1)
                last_user[("w_rg", g)] = ("rg", RT // 2 * (g + 1) - 1)

            def logits(h):
                if h == 0:
                    for ci in range(3, 7):
                        pe.wait_ge(*banks.read_out(("in2", ci)))
                    for hh in range(4):
                        pe.wait_ge(*banks.read_out(("k2", hh)))
                    for t in range(NT):
                        for g in range(2):
                            pe.wait_ge(*banks.read_out(("v2", t, g)))
                o = banks.new(("l2", h))
                pe.wait_ge(*banks.free(("l2", h)))
                for t in range(NT):
                    last = mm(o[:, S * t:S * t + S], q2[:, h, P * t:P * t + P], k2[:, h, :], start=True, stop=True)
                last.then_inc(banks.when_full(("l2", h)), 1)

            def prob_turn2(h):
                o = banks.new(("p2T", h))
                pe.wait_ge(*banks.free(("p2T", h)))
                pe.wait_ge(prob2_ready, h + 1)
                for s in range(NT):
                    for t in range(NT):
                        last = flip(o[:, S * s + P * t:S * s + P * t + P], prob2[:, h % 2, t, P * s:P * s + P])
                last.then_inc(banks.when_full(("p2T", h)), 1)

            def values2(h):
                o = banks.new(("att", h))
                pe.wait_ge(*banks.free(("att", h)))
                pe.wait_ge(*banks.read_out(("p2T", h)))
                for s in range(NT):
                    last = mm(o[:, 0:S], v2[:, s, AD * h:AD * h + AD], pT2[:, h % 2, s, :], start=s == 0, stop=s == NT - 1)
                last.then_inc(banks.when_full(("att", h)), 1)

            for n in range(AH + 2):
                if n < AH:
                    logits(n)
                if 1 <= n <= AH:
                    prob_turn2(n - 1)
                if n >= 2:
                    values2(n - 2)
                if n < 8:
                    project(17 + n)
            for c in range(KT // 2):
                o = banks.new(("ya", c))
                pe.wait_ge(*banks.free(("ya", c)))
                for m in range(2):
                    pe.wait_ge(*arrived(("w_rnn_out", 2 * c + m)))
                    w = chunk(("w_rnn_out", 2 * c + m))[:, 0:RT * P].rearrange("p (k n) -> p k n", k=RT)
                    for k in range(RT):
                        pe.wait_ge(gh_ready, k + 1)
                        last = mm(o[:, S * m:S * m + S], w[:, k, :], gr[:, k, :], start=k == 0, stop=k == RT - 1)
                    last_user[("w_rnn_out", 2 * c + m)] = ("ya", c)
                last.then_inc(banks.when_full(("ya", c)), 1)
            for h in range(AH):
                pe.wait_ge(*banks.read_out(("att", h)))
            for c in range(KT // 2):
                o = banks.new(("yb", c))
                pe.wait_ge(*banks.free(("yb", c)))
                pe.wait_ge(*arrived(("w_att_out", c)))
                w = chunk(("w_att_out", c)).rearrange("p (k n) -> p k n", k=AH)
                for m in range(2):
                    for k in range(AH):
                        last = mm(o[:, S * m:S * m + S], w[:, k, P * m:P * m + P], attT[:, k, :], start=k == 0, stop=k == AH - 1)
                last_user[("w_att_out", c)] = ("yb", c)
                last.then_inc(banks.when_full(("yb", c)), 1)
            row_out("b_gate1", diag2)
            pe.wait_ge(mix2_ready, KT // 2)
            for c in range(4):
                pe.wait_ge(*arrived(("w_out_2", c)))
                w = chunk(("w_out_2", c)).rearrange("p (k n) -> p k n", k=KT)
                o = banks.new(("wo2", c))
                pe.wait_ge(*banks.free(("wo2", c)))
                for t in range(NT):
                    for k in range(KT):
                        last = mm(o[:, 256 * t:256 * t + 256], mixT2[:, k, P * t:P * t + P], w[:, k, :], start=k == 0, stop=k == KT - 1)
                last.then_inc(banks.when_full(("wo2", c)), 1)
                last_user[("w_out_2", c)] = ("wo2", c)
            for tag in ("b_scale2", "b_shift2", "b_gate2"):
                row_out(tag, diag2)
            for kk in range(4):
                o = banks.new(("u2T", kk))
                pe.wait_ge(*banks.free(("u2T", kk)))
                pe.wait_ge(u2_ready, NT)
                for c in range(2):
                    for t in range(NT):
                        last = flip(o[:, S * c + P * t:S * c + P * t + P], u2[:, t, P * (2 * kk + c):P * (2 * kk + c) + P])
                last.then_inc(banks.when_full(("u2T", kk)), 1)
            o = banks.new("rt2")
            pe.wait_ge(*banks.free("rt2"))
            pe.wait_ge(wrt2_loaded, 16)
            for kk in range(4):
                pe.wait_ge(*banks.read_out(("u2T", kk)))
            NE = NG2 + E2
            for t in range(NT):
                for k in range(KT):
                    last = mm(o[:, NE * t:NE * t + NE], u2T[:, k, P * t:P * t + P], w_rt2[:, k, :], start=k == 0, stop=k == KT - 1)
            last.then_inc(banks.when_full("rt2"), 1)
            o = banks.new("pos2")
            pe.wait_ge(*banks.free("pos2"))
            pe.wait_ge(masks_ready, 1)
            mm(o[:, 0:E2], K("tri_f"), masks[:, 0, :], start=True, stop=True)
            mm(o[:, E2:2 * E2], ones, masks[:, 0, :], start=True, stop=False)
            mm(o[:, E2:2 * E2], K("tri_f"), masks[:, 1, :], start=False, stop=True)
            mm(o[:, 2 * E2:3 * E2], ones, masks[:, 0, :], start=True, stop=False)
            last = mm(o[:, 2 * E2:3 * E2], ones, masks[:, 1, :], start=False, stop=True)
            last.then_inc(banks.when_full("pos2"), 1)
            for b in range(8):
                pe.wait_ge(*banks.last(b))
            for free in (n_gathered, n_turned, n_spread):
                pe.sem_inc(free, 1)
            gather2(pe, 0)
            turn_tokens2(pe, 0)
            pair2_tensor(pe, 0, first=True)
            with pe.Fori(1, E2 // 2 - 1) as j:
                pair2_tensor(pe, j)
            pair2_tensor(pe, E2 // 2 - 1, final=True)
            for t in range(NT):
                spread_out2(pe, E2 - 1, 1, t)
            pe.wait_ge(flag_ready, 1)
            more = pe.value_load(flag[0:1, 0:1], min_val=0, max_val=S)
            with pe.If(more > CAP2):
                with pe.Fori(1, PASSES2) as p:
                    gather2(pe, 32 * p)
                    turn_tokens2(pe, 32 * p)
                    pair2_tensor(pe, 16 * p, first=True)
                    with pe.Fori(1, E2 // 2 - 1) as j:
                        pair2_tensor(pe, 16 * p + j)
                    pair2_tensor(pe, 16 * p + (E2 // 2 - 1), final=True)
                    for t in range(NT):
                        spread_out2(pe, 32 * p + (E2 - 1), 1, t)

        block = ctx.enter_context(nc.Block())

        @block.tensor
        def _(pe):
            mm = nc.tensor.matmul

            def flip(out_, in_, n=P):
                return nc.tensor.transpose(out_, in_, ident[0:n, 0:n])

            def mod_pair(b, p):
                key = ("mod", b, p)
                t = banks.new(key)
                pe.wait_ge(*banks.free(key))
                for i in range(2):
                    c = 2 * p + i
                    name = ("w_mod", "w_mod_2")[b]
                    pe.wait_ge(*arrived((name, c)))
                    w = chunk((name, c)).rearrange("p (k n) -> p k n", k=KT)
                    last_user[(name, c)] = key
                    for k2 in range(2):
                        for j in range(4):
                            mm(t[32 * j:32 * j + 32, 256 * i:256 * i + 256], svec[:, b, 2 * j + k2, :], w[:, 2 * j + k2, :],
                               start=k2 == 0, stop=k2 == 1 and j > 0)
                    last = mm(t[0:32, 256 * i:256 * i + 256], ident[0:24, c:c + 1].to_broadcast([24, 32]),
                              bmod[0:24, 256 * b:256 * b + 256], start=False, stop=True)
                last.then_inc(banks.when_full(key), 1)

            def mod_turn(b, p):
                t = banks.new(("modT", b, p))
                pe.wait_ge(*banks.free(("modT", b, p)))
                pe.wait_ge(*banks.read_out(("mod", b, p)))
                for q in range(4):
                    last = mm(t[:, 2 * q:2 * q + 2], mpart[:, p % 2, P * q:P * q + P], K("pick"), start=True, stop=True)
                last.then_inc(banks.when_full(("modT", b, p)), 1)

            def row_out(tag, diag=diag):
                for g in range(2):
                    o = banks.new(("row", tag, g))
                    pe.wait_ge(*banks.free(("row", tag, g)))
                    pe.wait_ge(diag_ready, 2 * ROWS.index(tag) + g + 1)
                    mm(o[:, :], ones, diag.rearrange("p c n -> p (c n)"), start=True, stop=True).then_inc(banks.when_full(("row", tag, g)), 1)

            for b in range(8):
                pe.sem_inc(banks.emptied[b], 1)
            pe.wait_ge(consts_loaded, 16)
            pe.wait_ge(svec_ready, 1)
            pe.wait_ge(bmod_loaded, 32)
            mod_pair(0, 0)
            mod_pair(0, 1)
            mod_turn(0, 0)
            for t in range(4):
                pe.wait_ge(xn_ready, t + 1)
                for g in range(2):
                    o = banks.new(("xT", t, g))
                    pe.wait_ge(*banks.free(("xT", t, g)))
                    for c in range(4):
                        last = flip(o[:, P * c:P * c + P], xn[:, t, P * (4 * g + c):P * (4 * g + c) + P])
                    last.then_inc(banks.when_full(("xT", t, g)), 1)
            for p in range(2, 4):
                mod_pair(0, p)
                mod_turn(0, p - 1)
            mod_turn(0, 3)
            pe.wait_ge(ftw_loaded, 16)
            for k in range(2):
                o = banks.new(("ftw", k))
                pe.wait_ge(*banks.free(("ftw", k)))
                mm(o[:, 0:256], K("bd_cos"), ft_w[:, k, :], start=True, stop=True)
                last = mm(o[:, 256:512], K("bd_sin"), ft_w[:, k, :], start=True, stop=True)
                last.then_inc(banks.when_full(("ftw", k)), 1)
            pe.wait_ge(h_ready, 1)
            pe.wait_ge(wab_loaded, 16)
            for ci, name in enumerate(CHUNKS):
                pe.wait_ge(*arrived(("w_in", ci)))
                w = chunk(("w_in", ci)).rearrange("p (k n) -> p k n", k=KT)
                if name in TILES_OF:
                    for t in TILES_OF[name]:
                        o = banks.new(("in", name, t))
                        pe.wait_ge(*banks.free(("in", name, t)))
                        for k in range(KT):
                            last = mm(o[:, 0:256], h3[:, k, P * t:P * t + P], w[:, k, :], start=k == 0, stop=k == KT - 1)
                        last.then_inc(banks.when_full(("in", name, t)), 1)
                        last_user[("w_in", ci)] = ("in", name, t)
                else:
                    n0 = 0 if name in BOTH else S
                    for f in range(2):
                        o = banks.new(("in", name, f))
                        pe.wait_ge(*banks.free(("in", name, f)))
                        for k in range(KT):
                            last = mm(o[:, n0:512], w[:, k, P * f:P * f + P], h3[:, k, n0:512], start=k == 0, stop=k == KT - 1)
                        last.then_inc(banks.when_full(("in", name, f)), 1)
                        last_user[("w_in", ci)] = ("in", name, f)
                if name == "dn_q":
                    o = banks.new("ab")
                    pe.wait_ge(*banks.free("ab"))
                    for t in range(4):
                        for k in range(KT):
                            last = mm(o[:, 16 * t:16 * t + 16], h3[:, k, P * t:P * t + P], w_ab[:, k, :], start=k == 0, stop=k == KT - 1)
                    last.then_inc(banks.when_full("ab"), 1)
                if name == "na_v":
                    for t in range(4):
                        o = banks.new(("kv_tm", t))
                        pe.wait_ge(*banks.free(("kv_tm", t)))
                        pe.wait_ge(conv_silu, 4)
                        for c in range(4):
                            last = flip(o[:, P * c:P * c + P], conv_kv[:, c, t // 2, P * (t % 2):P * (t % 2) + P])
                        last.then_inc(banks.when_full(("kv_tm", t)), 1)
                    o = banks.new("q_tm")
                    pe.wait_ge(*banks.free("q_tm"))
                    pe.wait_ge(conv_silu, 6)
                    for t in range(NT):
                        for c in range(2):
                            last = flip(o[:, GW * t + P * c:GW * t + P * c + P], conv_q[:, c, P * t:P * t + P])
                    last.then_inc(banks.when_full("q_tm"), 1)
                if name == "df_v":
                    o = banks.new("gc")
                    pe.wait_ge(*banks.free("gc"))
                    pe.wait_ge(g_ready, 1)
                    for d in range(2):
                        last = mm(o[:, 16 * d:16 * d + 16], K(("tri_f", "tri_b")[d]), g_log[:, :, d, :], start=True, stop=True)
                    last.then_inc(banks.when_full("gc"), 1)
                    for t in range(4):
                        o = banks.new(("kqT", t))
                        pe.wait_ge(*banks.free(("kqT", t)))
                        pe.wait_ge(kq_normed, 1)
                        for c in range(2):
                            last = flip(o[:, P * c:P * c + P], kv_tm[:, t, P * c:P * c + P])
                        if t >= 2:
                            for c in range(2):
                                last = flip(o[:, 256 + P * c:256 + P * c + P], q_tm[:, t - 2, P * c:P * c + P])
                        last.then_inc(banks.when_full(("kqT", t)), 1)
            for q, buf in (("df_q", df_q), ("df_k", df_k)):
                for f in range(2):
                    o = banks.new(("rot", q, f))
                    pe.wait_ge(*banks.free(("rot", q, f)))
                    pe.wait_ge(*banks.read_out(("in", q, f)))
                    last = mm(o[:, 0:S], K("rope_r"), buf[:, f, :] if q == "df_q" else buf[:, f, S:2 * S], start=True, stop=True)
                    last.then_inc(banks.when_full(("rot", q, f)), 1)
            for f in range(2):
                o = banks.new(("fta", f))
                pe.wait_ge(*banks.free(("fta", f)))
                for t in range(NT):
                    pe.wait_ge(*banks.read_out(("in", "ft_u", 2 + t)))
                    last = mm(o[:, :], ft_u[:, t, P * f:P * f + P], K("dft")[:, 512 * t:512 * t + 512], start=t == 0, stop=t == NT - 1)
                last.then_inc(banks.when_full(("fta", f)), 1)
            for c in range(2):
                o = banks.new(("fto", c))
                pe.wait_ge(*banks.free(("fto", c)))
                n = 0
                for f in range(2):
                    pe.wait_ge(*banks.read_out(("fta", f)))
                    pe.wait_ge(*banks.read_out(("ftw", f)))
                    for i in range(2):
                        last = mm(o[:, 0:S], ft_wc[:, f, i, P * c:P * c + P], ft_a[:, f, S * i:S * i + S], start=n == 0, stop=n == 3)
                        n += 1
                last.then_inc(banks.when_full(("fto", c)), 1)
            def scores(i):
                kind, h, t = ATT[i]
                if kind == "na":
                    o = banks.new(("s", i, 0))
                    pe.wait_ge(*banks.free(("s", i, 0)))
                    if i == 0:
                        pe.wait_ge(na_bias_ready, 1)
                    for f in range(2):
                        pe.wait_ge(*banks.read_out(("in", "na_q", f)))
                        pe.wait_ge(*banks.read_out(("in", "na_k", f)))
                    mm(o[:, :], na_q[hpart(h), h // 2, P * t:P * t + P], na_k[hpart(h), h // 2, :], start=True, stop=False)
                    last = mm(o[:, S:2 * S], ident, na_bias[:, 2 * h + t, :], start=False, stop=True)
                    last.then_inc(banks.when_full(("s", i, 0)), 1)
                else:
                    if i == 8:
                        pe.wait_ge(roped, 4)
                    for m in range(2):
                        o = banks.new(("s", i, m))
                        pe.wait_ge(*banks.free(("s", i, m)))
                        rows_ = slice(64 * (h % 2) + 32 * m, 64 * (h % 2) + 32 * m + 32)
                        last = mm(o[:, :], df_q[rows_, h // 2, P * t:P * t + P], df_k[rows_, h // 2, :], start=True, stop=True)
                        last.then_inc(banks.when_full(("s", i, m)), 1)

            def prob_turn(i):
                o = banks.new(("pT", i))
                pe.wait_ge(*banks.free(("pT", i)))
                pe.wait_ge(prob_ready, i + 1)
                src = prob[:, (i % 2) if i < 8 else 2, :]
                for c in range(4):
                    last = flip(o[:, P * c:P * c + P], src[:, P * c:P * c + P])
                last.then_inc(banks.when_full(("pT", i)), 1)

            def values(i):
                kind, h, t = ATT[i]
                o = banks.new(("pv", i))
                pe.wait_ge(*banks.free(("pv", i)))
                pe.wait_ge(*banks.read_out(("pT", i)))
                if i == 0:
                    for name in ("na_v", "df_v"):
                        for u in range(4):
                            pe.wait_ge(*banks.read_out(("in", name, u)))
                v0 = (0 if kind == "na" else GW) + HD * h
                for c in range(4):
                    last = mm(o[:, 0:HD], pT[:, i % 2, c, :], v_tm[:, c, v0:v0 + HD], start=c == 0, stop=c == 3)
                last.then_inc(banks.when_full(("pv", i)), 1)

            def fill(n):
                if n < NA_N:
                    scores(n)
                if 1 <= n <= NA_N:
                    prob_turn(n - 1)
                if 2 <= n <= NA_N + 1:
                    values(n - 2)
                if n < len(PAIRS):
                    mod_pair(*PAIRS[n])
                if 1 <= n <= len(PAIRS):
                    mod_turn(*PAIRS[n - 1])

            n = 0
            for t in range(4):
                o = banks.new(("kk", t))
                pe.wait_ge(*banks.free(("kk", t)))
                for u in ([0, 1, 2, 3] if t == 0 else []):
                    pe.wait_ge(*banks.read_out(("kqT", u)))
                for h in (0, 2, 1, 3):
                    kT = kqT[hpart(h), t, h // 2, :]
                    last = mm(o[:, P * h:P * h + P], kT, kT, start=True, stop=True)
                    if h == 2:
                        last.then_inc(pe_step, 1)
                        pe.wait_ge(pe_step, pe_steps())
                last.then_inc(banks.when_full(("kk", t)), 1)
                if t >= 2:
                    o = banks.new(("qk", t))
                    pe.wait_ge(*banks.free(("qk", t)))
                    for h in (0, 2, 1, 3):
                        last = mm(o[:, P * h:P * h + P], kqT[hpart(h), t, h // 2, :], kqT[hpart(h), t, 2 + h // 2, :], start=True, stop=True)
                        if h == 2:
                            last.then_inc(pe_step, 1)
                            pe.wait_ge(pe_step, pe_steps())
                    last.then_inc(banks.when_full(("qk", t)), 1)
                for d in range(2):
                    o = banks.new(("gb", t, d))
                    pe.wait_ge(*banks.free(("gb", t, d)))
                    for h in range(H):
                        last = mm(o[:, P * h:P * h + P], g_log[:, t, d, h:h + 1].to_broadcast([P, P]), K(("tri_f", "tri_b")[d]), start=True, stop=True)
                    last.then_inc(banks.when_full(("gb", t, d)), 1)
                fill(n)
                for d in range(2):
                    o = banks.new(("lt", t, d))
                    pe.wait_ge(*banks.free(("lt", t, d)))
                    pe.wait_ge(lower_ready, G(t, d) + 1)
                    for h in range(H):
                        last = flip(o[:, P * h:P * h + P], solve[d][:, 0, h, :])
                    last.then_inc(banks.when_full(("lt", t, d)), 1)
                fill(n + 1)
                n += 2
                for lv in range(1, 7):
                    for d in range(2):
                        o = banks.new(("x", t, d, lv))
                        pe.wait_ge(*banks.free(("x", t, d, lv)))
                        if lv == 1:
                            pe.wait_ge(inverse_begun, 2 * G(t, d) + 2)
                            pe.wait_ge(*banks.read_out(("lt", t, d)))
                        else:
                            pe.wait_ge(*banks.read_out(("dt", t, d, lv - 1)))
                        for h in range(H):
                            last = mm(o[:, P * h:P * h + P], solve[d][:, 1, h, :], solve[d][:, 2, h, :], start=True, stop=True)
                        last.then_inc(banks.when_full(("x", t, d, lv)), 1)
                    if lv in FILL_LEVELS:
                        fill(n)
                        n += 1
                    for d in range(2):
                        if lv < 6:
                            o = banks.new(("dt", t, d, lv))
                            pe.wait_ge(*banks.free(("dt", t, d, lv)))
                            pe.wait_ge(*banks.read_out(("x", t, d, lv)))
                            if lv > 1:
                                pe.wait_ge(*banks.read_out(("dtt", t, d, lv - 1)))
                            for h in range(H):
                                last = mm(o[:, P * h:P * h + P], solve[d][:, 3, h, :], solve[d][:, 0, h, :], start=True, stop=True)
                            last.then_inc(banks.when_full(("dt", t, d, lv)), 1)
                        o = banks.new(("dtt", t, d, lv))
                        pe.wait_ge(*banks.free(("dtt", t, d, lv)))
                        pe.wait_ge(*banks.read_out(("x", t, d, lv)))
                        if lv > 1:
                            pe.wait_ge(*banks.read_out(("dtt", t, d, lv - 1)))
                        for h in range(H):
                            last = mm(o[:, P * h:P * h + P], solve[d][:, 0, h, :], solve[d][:, 3, h, :], start=True, stop=True)
                        last.then_inc(banks.when_full(("dtt", t, d, lv)), 1)
                for d in range(2):
                    o = banks.new(("uw", t, d))
                    pe.wait_ge(*banks.free(("uw", t, d)))
                    pe.wait_ge(*banks.read_out(("dtt", t, d, 6)))
                    pe.wait_ge(vk_ready, G(t, d) + 1)
                    for h in range(H):
                        mm(o[:, HD * h:HD * h + HD], solve[d][:, 3, h, :], vk[:, 0, h, :], start=True, stop=True)
                    for h in range(H):
                        last = mm(o[hpart(h), 256 + P * (h // 2):256 + P * (h // 2) + P], vk[:, 1, h, :], solve[d][:, 3, h, :], start=True, stop=True)
                    last.then_inc(banks.when_full(("uw", t, d)), 1)
            for step, d, t in ORDER:
                pe.wait_ge(*banks.read_out(("uw", t, d)))
                if step:
                    o = banks.new(("ws", step, d))
                    pe.wait_ge(*banks.free(("ws", step, d)))
                    pe.wait_ge(state_ready[d], step)
                    for h in (0, 2, 1, 3):
                        g = h // 2
                        last = mm(o[:, HD * h:HD * h + HD], uw[hpart(h), d, t, 256 + P * g:256 + P * g + P], state[hpart(h), d, g, :], start=True, stop=True)
                        if t >= 2:
                            last = mm(o[:, 256 + HD * h:256 + HD * h + HD], kqT[hpart(h), t, 2 + g, :], state[hpart(h), d, g, :], start=True, stop=True)
                        if h == 2:
                            last.then_inc(pe_step, 1)
                            pe.wait_ge(pe_step, pe_steps())
                    last.then_inc(banks.when_full(("ws", step, d)), 1)
                o = banks.new(("so", step, d))
                pe.wait_ge(*banks.free(("so", step, d)))
                pe.wait_ge(vnew_ready[d], step + 1)
                pe.wait_ge(kd_ready, G(t, d) + 1)
                if step < 3:
                    for h in range(H):
                        last = mm(o[hpart(h), HD * (h // 2):HD * (h // 2) + HD], kd[:, d, t, h, :], vnew[:, d, h, :], start=True, stop=True)
                if t >= 2:
                    pe.wait_ge(qk_ready, 2 * (t - 2) + d + 1)
                    for h in range(H):
                        last = mm(o[:, 256 + HD * h:256 + HD * h + HD], qk[:, d, t - 2, h, :], vnew[:, d, h, :], start=True, stop=True)
                last.then_inc(banks.when_full(("so", step, d)), 1)
                if d == 1:
                    fill(n)
                    n += 1
            assert n >= NA_N + 2 and n > len(PAIRS)
            row_out("gate1")
            for i in range(3):
                o = banks.new(("mixT", i))
                pe.wait_ge(*banks.free(("mixT", i)))
                pe.wait_ge(mix_ready, 3)
                for c in range(2):
                    for t in range(NT):
                        last = flip(o[:, S * c + P * t:S * c + P * t + P], mix[:, t, P * (2 * i + c):P * (2 * i + c) + P])
                last.then_inc(banks.when_full(("mixT", i)), 1)
            for i in range(3):
                pe.wait_ge(*banks.read_out(("mixT", i)))
            for c in range(2):
                pe.wait_ge(*banks.read_out(("fto", c)))
            for c in range(4):
                pe.wait_ge(*arrived(("w_out", c)))
                w = chunk(("w_out", c)).rearrange("p (k n) -> p k n", k=KT)
                for t in range(NT):
                    o = banks.new(("wo", c, t))
                    pe.wait_ge(*banks.free(("wo", c, t)))
                    for k in range(KT):
                        m = mixT[:, k, P * t:P * t + P] if k < 6 else ft_o[:, k - 6, P * t:P * t + P]
                        last = mm(o[:, 0:256], m, w[:, k, :], start=k == 0, stop=k == KT - 1)
                    last.then_inc(banks.when_full(("wo", c, t)), 1)
                last_user[("w_out", c)] = ("wo", c, 1)
            for tag in ("scale2", "shift2", "gate2"):
                row_out(tag)
            for t in range(NT):
                for g in range(2):
                    o = banks.new(("h2T", t, g))
                    pe.wait_ge(*banks.free(("h2T", t, g)))
                    pe.wait_ge(h2_ready, t + 1)
                    for c in range(4):
                        last = flip(o[:, P * c:P * c + P], h2[:, t, P * (4 * g + c):P * (4 * g + c) + P])
                    last.then_inc(banks.when_full(("h2T", t, g)), 1)
            o = banks.new("rt")
            pe.wait_ge(*banks.free("rt"))
            pe.wait_ge(wrt_loaded, 16)
            for t in range(NT):
                for g in range(2):
                    pe.wait_ge(*banks.read_out(("h2T", t, g)))
                for k in range(KT):
                    last = mm(o[:, E1 * t:E1 * t + E1], h2T[:, k, P * t:P * t + P], w_rt[:, k, :], start=k == 0, stop=k == KT - 1)
            last.then_inc(banks.when_full("rt"), 1)
            o = banks.new("affT")
            pe.wait_ge(*banks.free("affT"))
            pe.wait_ge(aff_ready, 1)
            for t in range(NT):
                last = flip(o[0:E1, P * t:P * t + P], rt[:, t, :])
            last.then_inc(banks.when_full("affT"), 1)
            o = banks.new("pgT")
            pe.wait_ge(*banks.free("pgT"))
            pe.wait_ge(choice_ready, 2)
            for i in range(2):
                for t in range(NT):
                    last = flip(o[:, 32 * i + 16 * t:32 * i + 16 * t + 16], aff[0:E1, 3 + i, P * t:P * t + P], E1)
            last.then_inc(banks.when_full("pgT"), 1)
            for b in range(8):
                pe.wait_ge(*banks.last(b))
            for free in (m_gathered, m_turned, m_spread):
                pe.sem_inc(free, 1)
            with pe.Fori(0, E1) as e:
                moe1_tensor(pe, e)
            block2_tensor(pe, flip, row_out)

        @block.sync
        def _(sp):
            for key, s, before in plan1:
                if before is not None:
                    sp.wait_ge(*banks.full(last_user[before]))
                sp.dma_start(slot(s)[:, 0:A[key[0]].shape[2]], A[key[0]][key[1]]).then_inc(loaded[s], 16)
            for n in range(SLOTS):
                if n == FRONT:
                    sp.wait_ge(mixers_done, 1)
                if n < FRONT:
                    sp.wait_ge(*banks.full(last_user[holder1[n]]))
                moe1_load(sp, 0, n)
            for n in range(SLOTS, 24):
                sp.wait_ge(m_chunk_used, n - SLOTS + 1)
                moe1_load(sp, 0, n)
            with sp.Fori(1, E1) as e:
                for n in range(24):
                    sp.wait_ge(m_chunk_used, 24 * e + (n - SLOTS + 1))
                    moe1_load(sp, e, n)
            for key, s, before in plan2:
                if before is not None:
                    sp.wait_ge(*banks.full(last_user[before]))
                else:
                    sp.wait_ge(m_chunk_used, 24 * E1 - SLOTS + s + 1)
                    if s == 0:
                        sp.wait_ge(block1_ready, 1)
                sp.dma_start(slot(s)[:, 0:A[key[0]].shape[2]], A[key[0]][key[1]]).then_inc(loaded[s], 16)
            for n in range(12):
                if n == FRONT:
                    sp.wait_ge(mixers2_done, 1)
                if n < FRONT:
                    sp.wait_ge(*banks.full(last_user[holder2[n]]))
                moe2_load(sp, 0, n)
            with sp.Fori(1, E2 // 2) as j:
                for n in range(12):
                    sp.wait_ge(n_chunk_used, 12 * j + (n - 11))
                    moe2_load(sp, j, n)
            sp.wait_ge(flag_ready, 1)
            more = sp.value_load(flag[0:1, 0:1], min_val=0, max_val=S)
            with sp.If(more > CAP2):
                with sp.Fori(1, PASSES2) as p:
                    with sp.Fori(0, E2 // 2) as j:
                        for n in range(12):
                            sp.wait_ge(n_chunk_used, 12 * (16 * p + j) + (n - 11))
                            moe2_load(sp, j, n)
            sp.wait_ge(out_ready, 1)
            for t in range(NT):
                sp.dma_start(out[0, P * t:P * t + P, :], x[:, t, :]).then_inc(stored, 16)
            sp.wait_ge(stored, 32)

        @block.scalar
        def _(act):
            def copy_out(key, dst, src=lambda o: o, scale=1.0, func=ACT.Copy):
                act.wait_ge(*banks.full(key))
                o = banks.tile(key)
                act.activation(dst, src(o), func, scale=scale).then_inc(banks.when_read(key), 1)

            act.dma_start(sml, A["small"]).then_inc(small_loaded, 16)
            for b in range(2):
                act.dma_start(bmod[0:24, 256 * b:256 * b + 256], A["b_mod"][b]).then_inc(bmod_loaded, 16)
            act.dma_start(cst, A["const1"]).then_inc(consts_loaded, 16)
            for t in range(NT):
                act.dma_start(ctx_in[:, t, :], A["ctx"][t]).then_inc(ctx_loaded, 16)
            act.dma_start(x[:, 0, :], A["x"][0]).then_inc(x_loaded, 16)
            act.dma_start(x[:, 1, :], A["x"][1]).then_inc(x_loaded, 16)
            act.dma_start(w_ab, A["w_ab"]).then_inc(wab_loaded, 16)
            act.dma_start(ft_w, A["ft_w"]).then_inc(ftw_loaded, 16)
            act.wait_ge(small_loaded, 16)
            act.wait_ge(svec_zero, 1)
            for name, b, m in (("c", 0, 0), ("c_ctx", 0, 1)):
                act.activation(svec[:, b, :, m], M(name), ACT.Silu).then_inc(act_step, 1)
                act.wait_ge(act_step, act_steps())
            act.activation(svec[:, 1, :, 0], M("c_2"), ACT.Silu).then_inc(svec_ready, 1)
            act.wait_ge(ctx_loaded, 32)
            for t in range(NT):
                act.activation(xn[:, t, :], ctx_in[:, t, :], ACT.Square, accum_out=stat[:, t:t + 1]).then_inc(act_step, 1)
                act.wait_ge(act_step, act_steps())
            act.wait_ge(x_loaded, 32)
            for t in range(NT):
                act.activation(xn[:, 2 + t, :], x[:, t, :], ACT.Square, accum_out=stat[:, 2 + t:3 + t]).then_inc(act_step, 1)
                act.wait_ge(act_step, act_steps())
            act.sem_inc(squares_ready, 1)
            def mod_out(b, p, i):
                if i >= 2:
                    act.wait_ge(*banks.full(MODT[i - 2]))
                copy_out(("mod", b, p), mpart[:, i % 2, :])

            MODT = [("modT", 0, p) for p in range(4)] + [("modT", *bp) for bp in PAIRS]
            for p in range(2):
                mod_out(0, p, p)
            for t in range(4):
                for g in range(2):
                    copy_out(("xT", t, g), h3[:, 4 * g:4 * g + 4, P * t:P * t + P], lambda o: o.rearrange("p (c n) -> p c n", c=4))
            for p in range(2, 4):
                mod_out(0, p, p)
            for k in range(2):
                copy_out(("ftw", k), ft_wc[:, k, :, :], lambda o: o.rearrange("p (i n) -> p i n", i=2))
            act.dma_start(na_bias, A["na_bias"]).then_inc(na_bias_loaded, 16)
            act.wait_ge(pad_zero, 1)
            for name in CHUNKS:
                if name in TILES_OF:
                    for t in TILES_OF[name]:
                        key = ("in", name, t)
                        lo = lambda o: o[:, 0:256]
                        if name == "na_v":
                            copy_out(key, v_tm[:, t, 0:GW], lo)
                        elif name == "df_v":
                            copy_out(key, v_tm[:, t, GW:2 * GW], lo)
                        elif name == "dn_gate":
                            copy_out(key, gate_tm[:, t - 2, :], lo, func=ACT.Silu)
                        else:
                            copy_out(key, ft_u[:, t - 2, :], lo)
                    if name == "na_v":
                        for t in range(4):
                            copy_out(("kv_tm", t), kv_tm[:, t, :])
                        copy_out("q_tm", q_tm, lambda o: o.rearrange("p (t n) -> p t n", t=NT))
                    if name == "df_v":
                        act.wait_ge(*banks.full("gc"))
                        o = banks.tile("gc")
                        src = o[:, 0:32].rearrange("p (d t h) -> p d t h", d=2, t=4)
                        act.activation(egc, src, ACT.Exp).then_inc(act_step, 1)
                        act.wait_ge(act_step, act_steps())
                        act.activation(gcum, src, ACT.Copy).then_inc(banks.when_read("gc"), 1)
                        for t in range(4):
                            n = 4 if t >= 2 else 2
                            copy_out(("kqT", t), kqT[:, t, 0:n, :], lambda o: o[:, 0:P * n].rearrange("p (c q) -> p c q", c=n))
                    continue
                for f in range(2):
                    key = ("in", name, f)
                    two = lambda o: o.rearrange("p (s t) -> p s t", s=2)
                    if name == "dn_k":
                        copy_out(key, pad_kv[:, f, :, 2:2 + S], two)
                    elif name == "dn_v":
                        copy_out(key, pad_kv[:, 2 + f, :, 2:2 + S], two)
                    elif name == "dn_q":
                        copy_out(key, pad_q[:, f, 2:2 + S], lambda o: o[:, S:2 * S])
                    elif name == "na_q":
                        copy_out(key, na_q[:, f, :], lambda o: o[:, S:2 * S], scale=HD ** -0.5)
                    elif name == "na_k":
                        copy_out(key, na_k[:, f, :])
                    elif name == "df_q":
                        copy_out(key, df_q[:, f, :], lambda o: o[:, S:2 * S])
                    elif name == "df_k":
                        copy_out(key, df_k[:, f, :])
                    if name == "df_q":
                        for c in (2 * f, 2 * f + 1):
                            act.wait_ge(conv_ready, c + 1)
                            act.activation(conv_kv[:, c], conv_kv[:, c], ACT.Silu).then_inc(conv_silu, 1)
                    if name == "df_k":
                        act.wait_ge(conv_ready, 4 + f + 1)
                        act.activation(conv_q[:, f], conv_q[:, f], ACT.Silu).then_inc(conv_silu, 1)
                if name == "df_k":
                    act.wait_ge(softplus_arg, 1)
                    act.activation(sp[:, 1, :], sp[:, 1, :], ACT.Exp, scale=-1.0).then_inc(act_step, 1)
                    act.wait_ge(act_step, act_steps())
                    act.activation(sp[:, 5, 0:8], M("a_log"), ACT.Exp).then_inc(act_step, 1)
                    act.wait_ge(act_step, act_steps())
                    act.activation(beta, ab[:, :, 8:16].rearrange("p t (d h) -> p t d h", d=2), ACT.Exp, scale=-1.0).then_inc(act_step, 1)
                    act.wait_ge(act_step, act_steps())
                    act.activation(nlam[:, 2:4], nlam[:, 0:2], ACT.Exp).then_inc(softplus_exp, 1)
            for f in range(2):
                copy_out(("fta", f), ft_a[:, f, :])
            for c in range(2):
                copy_out(("fto", c), ft_o[:, c, :], lambda o: o[:, 0:S])

            def attend(n):
                if n < NA_N:
                    kind = ATT[n][0]
                    act.wait_ge(smax_ready, n + 1)
                    if kind == "na":
                        if n >= 2:
                            act.wait_ge(*banks.full(("pT", n - 2)))
                        act.wait_ge(*banks.full(("s", n, 0)))
                        o = banks.tile(("s", n, 0))
                        act.activation(prob[:, n % 2, :], o, ACT.Exp, bias=smax[:, 0, 4 * (n % 4):4 * (n % 4) + 1],
                                       accum_out=smax[:, 1, 4 * (n % 4):4 * (n % 4) + 1]).then_inc(act_step, 1)
                        act.wait_ge(act_step, act_steps())
                        act.sem_inc(banks.when_read(("s", n, 0)), 1)
                        act.sem_inc(prob_exp, 1)
                    else:
                        for m in range(2):
                            if n >= 8 and m == 0:
                                act.wait_ge(prob_ready, n)
                                if n == 8:
                                    act.wait_ge(*banks.full(("pT", 7)))
                            act.wait_ge(*banks.full(("s", n, m)))
                            o = banks.tile(("s", n, m))
                            act.activation(prob[:, m, :], o, ACT.Exp, scale=32 ** -0.5, bias=smax[:, 0, 4 * (n % 4) + m:4 * (n % 4) + m + 1],
                                           accum_out=smax[:, 1, 4 * (n % 4) + m:4 * (n % 4) + m + 1]).then_inc(act_step, 1)
                            act.wait_ge(act_step, act_steps())
                            act.sem_inc(banks.when_read(("s", n, m)), 1)
                        act.sem_inc(prob_exp, 1)
                if 1 <= n <= NA_N:
                    if n - 1 >= 2:
                        act.wait_ge(*banks.full(("pv", n - 3)))
                    copy_out(("pT", n - 1), pT[:, (n - 1) % 2], lambda o: o.rearrange("p (c q) -> p c q", c=4))
                if 2 <= n <= NA_N + 1:
                    kind, h, t = ATT[n - 2]
                    c0 = (0 if kind == "na" else 512) + HD * h
                    copy_out(("pv", n - 2), mix[:, t, c0:c0 + HD], lambda o: o[:, 0:HD],
                             scale=smax[:, 2, 4 * ((n - 2) % 4):4 * ((n - 2) % 4) + 1] if kind == "na" else 1.0)
                if n < len(PAIRS):
                    mod_out(*PAIRS[n], 4 + n)

            n = 0
            for t in range(4):
                copy_out(("kk", t), kk_sb, lambda o: o.rearrange("p (h n) -> p h n", h=H))
                for d in range(2):
                    g = G(t, d)
                    act.wait_ge(decay_arg, g + 1)
                    if t >= 2:
                        act.activation(etm, etm, ACT.Exp).then_inc(act_step, 1)
                        act.wait_ge(act_step, act_steps())
                    act.activation(emat, emat, ACT.Exp, scale=-1.0).then_inc(decay_exp, 1)
                    act.activation(ekd[:, d, t, :], ekd[:, d, t, :], ACT.Exp).then_inc(act_step, 1)
                    act.wait_ge(act_step, act_steps())
                    act.activation(gls[0:64, d, t, :], glast[0:64, d, t, 0:4:2], ACT.Exp).then_inc(act_step, 1)
                    act.wait_ge(act_step, act_steps())
                    act.activation(gls[64:128, d, t, :], glast[64:128, d, t, 1:4:2], ACT.Exp).then_inc(gls_ready, 1)
                for d in range(2):
                    copy_out(("lt", t, d), solve[d][:, 1], lambda o: o.rearrange("p (h n) -> p h n", h=H))
                attend(n)
                attend(n + 1)
                n += 2
                for lv in FILL_LEVELS:
                    attend(n)
                    n += 1
                for d in range(2):
                    copy_out(("uw", t, d), uw[:, d, t, :])
            for step in range(4):
                attend(n)
                n += 1
            for tag in ["gate1"]:
                for g in range(2):
                    copy_out(("row", tag, g), rows[:, 0, 512 * g:512 * g + 512])
            act.dma_start(acc[:, 0, :], A["norm2_g"].to_broadcast([P, D])).then_inc(gain_loaded, 16)
            act.dma_start(w_rt, A["w_router"]).then_inc(wrt_loaded, 16)
            for i in range(3):
                copy_out(("mixT", i), mixT[:, 2 * i:2 * i + 2, :], lambda o: o.rearrange("p (c t) -> p c t", c=2))
            for i, tag in ((1, "scale2"), (2, "shift2"), (0, "gate2")):
                if tag == "gate2":
                    act.wait_ge(x1_ready, 2)
                for g in range(2):
                    copy_out(("row", tag, g), rows[:, i, 512 * g:512 * g + 512])
                if tag == "shift2":
                    for t in range(NT):
                        act.wait_ge(x1_ready, t + 1)
                        ins = act.activation(h2[:, t, :], x[:, t, :], ACT.Square, accum_out=rstat[:, t:t + 1])
                        ins.then_inc(act_step, 1)
                        act.wait_ge(act_step, act_steps())
                    act.sem_inc(squares_ready, 1)
            for t in range(NT):
                for g in range(2):
                    copy_out(("h2T", t, g), h2T[:, 4 * g:4 * g + 4, P * t:P * t + P], lambda o: o.rearrange("p (c n) -> p c n", c=4))
            for t in range(NT):
                act.wait_ge(rt_max, t + 1)
                act.wait_ge(*banks.full("rt"))
                o = banks.tile("rt")
                act.activation(rt[:, t, :], o[:, E1 * t:E1 * t + E1], ACT.Exp, bias=rstat[:, 4 + t:5 + t], accum_out=rstat[:, 6 + t:7 + t]).then_inc(act_step, 1)
                act.wait_ge(act_step, act_steps())
            act.sem_inc(banks.when_read("rt"), 1)
            act.sem_inc(rt_exp, 1)
            act.wait_ge(h2_ready, 2)
            act.dma_start(rows[:, 1, :], A["final_norm_g"].to_broadcast([P, D])).then_inc(gain_loaded, 16)
            act.sem_inc(m_xg, 1)
            act.sem_inc(m_hidT, 1)
            act.sem_inc(m_y, 1)
            with act.Fori(0, E1) as e:
                moe1_scalar(act, e)
            for t in range(NT):
                act.wait_ge(x2_ready, t + 1)
                act.activation(h2[:, t, :], x[:, t, :], ACT.Square, accum_out=rstat[:, 10 + t:11 + t]).then_inc(act_step, 1)
                act.wait_ge(act_step, act_steps())
            act.sem_inc(squares_ready, 1)
            act.wait_ge(block1_ready, 1)
            act.dma_start(c2, A["const2"]).then_inc(const2_loaded, 16)
            for t in range(NT):
                act.activation(xn2[:, t, :], x[:, t, :], ACT.Square, accum_out=stat2[:, t:t + 1]).then_inc(act_step, 1)
                act.wait_ge(act_step, act_steps())
            act.sem_inc(squares_ready, 1)
            act.wait_ge(lru_arg, 1)
            act.activation(nsp[:, 1, :], nsp[:, 1, :], ACT.Exp, scale=-1.0).then_inc(act_step, 1)
            act.wait_ge(act_step, act_steps())
            act.sem_inc(lru_exp, 1)

            def project_out(ci):
                key, kind = ("in2", ci), KIND2[ci]
                n = 2 * (ci - FIRST2[kind])
                two = lambda o: o.rearrange("p (c t) -> p c t", c=2)
                if kind == "ckv":
                    act.wait_ge(*banks.full(key))
                    o = banks.tile(key)
                    for t in range(NT):
                        act.activation(ckv[:, t, :], o[:, 256 * t:256 * t + 256], ACT.Copy).then_inc(act_step, 1)
                        act.wait_ge(act_step, act_steps())
                    for t in range(NT):
                        act.activation(relu[:, t, :], o[:, 256 * t:256 * t + 256], ACT.Square, accum_out=stat2[:, 4 + t:5 + t]).then_inc(act_step, 1)
                        act.wait_ge(act_step, act_steps())
                    act.sem_inc(banks.when_read(key), 1)
                    act.sem_inc(squares_ready, 1)
                elif kind == "qi":
                    copy_out(key, qi[:, n:n + 2, :], two)
                elif kind == "q":
                    copy_out(key, q2[:, n:n + 2, :], two)
                elif kind == "xr":
                    copy_out(key, xr[:, n:n + 2, LEAD:], two)
                else:
                    copy_out(key, gr[:, n:n + 2, :], two, func=ACT.Gelu_apprx_tanh)

            for ci in range(3):
                project_out(ci)
            act.wait_ge(*banks.full("ki"))
            o = banks.tile("ki")
            act.activation(ki, o[:, 0:S], ACT.Copy).then_inc(act_step, 1)
            act.wait_ge(act_step, act_steps())
            act.activation(wi, o[:, S:S + NT * IH].rearrange("p (t h) -> p t h", t=NT), ACT.Copy).then_inc(banks.when_read("ki"), 1)
            for n, key in enumerate(IDXB):
                if n:
                    act.wait_ge(relu_used, n)
                else:
                    act.wait_ge(ckv_normed, 1)
                copy_out(("idx", *key), relu, lambda o: o.rearrange("p (i n) -> p i n", i=2), func=ACT.Relu)
            copy_out("ckvT", ckvT, lambda o: o.rearrange("p (r t) -> p r t", r=2))
            for ci in range(3, 7):
                project_out(ci)
            for hh in range(AH // 2):
                copy_out(("k2", hh), k2[:, 2 * hh:2 * hh + 2, :], lambda o: o.rearrange("p (c t) -> p c t", c=2))
            for t in range(NT):
                for g in range(2):
                    copy_out(("v2", t, g), v2[:, t, 512 * g:512 * g + 512])
            act.wait_ge(xr_zero, 1)
            for ci in range(7, 17):
                project_out(ci)
            for n in range(RT):
                act.wait_ge(*banks.full(("rg", n)))
                o = banks.tile(("rg", n))
                act.activation(rb[:, n, :], o[:, 0:S], ACT.Sigmoid, bias=M("rg_a")[:, n:n + 1]).then_inc(act_step, 1)
                act.wait_ge(act_step, act_steps())
                act.activation(th[:, n, :], o[:, S:2 * S], ACT.Sigmoid, bias=M("rg_x")[:, n:n + 1]).then_inc(act_step, 1)
                act.wait_ge(act_step, act_steps())
                act.sem_inc(banks.when_read(("rg", n)), 1)
                act.sem_inc(rg_ready, 1)
            flat = lambda v: v.rearrange("p c t -> p (c t)")
            act.wait_ge(la_ready, 1)
            act.activation(flat(th), flat(la), ACT.Tanh).then_inc(act_step, 1)
            act.wait_ge(act_step, act_steps())
            act.activation(flat(la), flat(la), ACT.Exp).then_inc(decay2_ready, 1)
            def attend2(n):
                if 1 <= n <= AH:
                    if n >= 3:
                        act.wait_ge(*banks.full(("att", n - 3)))
                    copy_out(("p2T", n - 1), pT2[:, (n - 1) % 2], lambda o: o.rearrange("p (s q) -> p s q", s=NT))
                if n >= 2:
                    copy_out(("att", n - 2), attT[:, n - 2, :], lambda o: o[:, 0:S])
                if n < AH:
                    act.wait_ge(smax2_ready, n + 1)
                    for t in range(NT):
                        c = 3 * (n % 4)
                        act.activation(prob2[:, n % 2, t, :], prob2[:, n % 2, t, :], ACT.Exp, bias=smax2[:, c, t:t + 1],
                                       accum_out=smax2[:, c + 1, t:t + 1]).then_inc(act_step, 1)
                        act.wait_ge(act_step, act_steps())
                    act.sem_inc(exp2_ready, 1)
                if n < 8:
                    copy_out(("in2", 17 + n), mg[:, 2 * n:2 * n + 2, :], lambda o: o.rearrange("p (c t) -> p c t", c=2))

            for n in range(AH + 2):
                attend2(n)
                if n == 2:
                    act.wait_ge(lru_var, 1)
                    act.activation(flat(th), flat(th), ACT.Sqrt).then_inc(lru_std, 1)
            for c in range(16):
                act.activation(mg[:, c, :], mg[:, c, :], ACT.Sigmoid).then_inc(act_step, 1)
                act.wait_ge(act_step, act_steps())
                act.sem_inc(mg_ready, 1)
            for g in range(2):
                copy_out(("row", "b_gate1", g), rows2[:, 0, 512 * g:512 * g + 512])
            act.dma_start(acc2[:, 0, :], A["norm2_g_2"].to_broadcast([P, D])).then_inc(gain2_loaded, 16)
            act.dma_start(w_rt2, A["w_router_2"]).then_inc(wrt2_loaded, 16)
            for i, tag in ((1, "b_scale2"), (2, "b_shift2"), (0, "b_gate2")):
                if tag == "b_gate2":
                    act.wait_ge(x3_ready, 1)
                for g in range(2):
                    copy_out(("row", tag, g), rows2[:, i, 512 * g:512 * g + 512])
                if tag == "b_shift2":
                    act.wait_ge(x3_ready, 1)
                    for t in range(NT):
                        act.activation(u2[:, t, :], x[:, t, :], ACT.Square, accum_out=rs2[:, t:t + 1]).then_inc(act_step, 1)
                        act.wait_ge(act_step, act_steps())
                    act.sem_inc(squares_ready, 1)
            for kk in range(4):
                copy_out(("u2T", kk), u2T[:, 2 * kk:2 * kk + 2, :], lambda o: o.rearrange("p (c t) -> p c t", c=2))
            act.wait_ge(u2_ready, NT)
            act.dma_start(rows2[:, 1, :], A["final_g_2"].to_broadcast([P, D])).then_inc(gain2_loaded, 16)
            act.wait_ge(group_max, 1)
            for t in range(NT):
                act.activation(rt2[:, 3, t, 0:NG2], lg[:, t, 0:NG2], ACT.Exp, bias=rs2[:, 8 + t:9 + t], accum_out=rs2[:, 10 + t:11 + t]).then_inc(act_step, 1)
                act.wait_ge(act_step, act_steps())
            act.activation(rs2[:, 14:16], rs2[:, 12:14], ACT.Exp).then_inc(act_step, 1)
            act.wait_ge(act_step, act_steps())
            act.sem_inc(route_exp, 1)
            for free in (n_xg, n_hidT, n_y):
                act.sem_inc(free, 1)
            for b in range(8):
                act.wait_ge(*banks.last(b))
            read_gathered2(act, 0, 0)
            pair2_scalar(act, 0, first=True)
            with act.Fori(1, E2 // 2 - 1) as j:
                pair2_scalar(act, j)
            pair2_scalar(act, E2 // 2 - 1, final=True)
            act.wait_ge(flag_ready, 1)
            more = act.value_load(flag[0:1, 0:1], min_val=0, max_val=S)
            with act.If(more > CAP2):
                with act.Fori(1, PASSES2) as p:
                    act.wait_ge(n_spread, 64 * p + 1)
                    read_gathered2(act, 32 * p, 0)
                    pair2_scalar(act, 16 * p, first=True)
                    with act.Fori(1, E2 // 2 - 1) as j:
                        pair2_scalar(act, 16 * p + j)
                    pair2_scalar(act, 16 * p + (E2 // 2 - 1), final=True)
            for t in range(NT):
                act.wait_ge(x4_ready, t + 1)
                act.activation(u2[:, t, :], x[:, t, :], ACT.Square, accum_out=rs2[:, 20 + t:21 + t]).then_inc(act_step, 1)
                act.wait_ge(act_step, act_steps())
            act.sem_inc(squares_ready, 1)

        @block.vector
        def _(dve):
            V = nc.vector
            V.memset(svec, 0.0).then_inc(dve_step, 1)
            dve.wait_ge(dve_step, dve_steps())
            dve.sem_inc(svec_zero, 1)
            V.memset(half, -0.5).then_inc(dve_step, 1)
            dve.wait_ge(dve_step, dve_steps())
            dve.sem_inc(half_ready, 1)
            V.memset(padf, 0.0).then_inc(dve_step, 1)
            dve.wait_ge(dve_step, dve_steps())
            dve.sem_inc(pad_zero, 1)
            dve.wait_ge(rstd_ready, 1)
            for t in range(4):
                src = ctx_in[:, t, :] if t < 2 else x[:, t - 2, :]
                V.tensor_scalar(xn[:, t, :], src, stat[:, 4 + t:5 + t], None, ALU.mult).then_inc(xn_ready, 1)

            def mod_in(b, p):
                dve.wait_ge(*banks.full(("modT", b, p)))
                o = banks.tile(("modT", b, p))
                V.tensor_copy(mfm[:, b, 4 * p:4 * p + 4, :], o[:, 0:8].rearrange("p (k m) -> p k m", m=2)).then_inc(banks.when_read(("modT", b, p)), 1)
                dve.wait_ge(*banks.read_out(("modT", b, p)))

            for p in range(4):
                mod_in(0, p)
            for m in range(2):
                V.scalar_tensor_tensor(scale_fm[:, m, :], mfm[:, 0, KT:2 * KT, m], 1.0, M("norm1"), ALU.add, ALU.mult).then_inc(dve_step, 1)
                dve.wait_ge(dve_step, dve_steps())
            for t in range(4):
                for g in range(2):
                    dve.wait_ge(*banks.read_out(("xT", t, g)))
            for k in range(KT):
                for m in range(2):
                    sl = h3[:, k, S * (1 - m):S * (2 - m)]
                    V.tensor_scalar(sl, sl, scale_fm[:, m, k:k + 1], mfm[:, 0, k, m:m + 1], ALU.mult, ALU.add).then_inc(dve_step, 1)
                    dve.wait_ge(dve_step, dve_steps())
            dve.sem_inc(h_ready, 1)
            lw = M("df_lambda").rearrange("p (i n) -> p i n", i=4)
            for i in range(2):
                V.tensor_tensor(sp[:, i, :], lw[:, 2 * i, :], lw[:, 2 * i + 1, :], ALU.mult).then_inc(dve_step, 1)
                dve.wait_ge(dve_step, dve_steps())
                V.tensor_reduce(nlam[:, i:i + 1], sp[:, i, :], AX.X, ALU.add).then_inc(dve_step, 1)
                dve.wait_ge(dve_step, dve_steps())
            cw = M("conv").rearrange("p (c j) -> p c j", j=CONV)
            for c in range(6):
                name = ("dn_k", "dn_v", "dn_q")[c // 2]
                dve.wait_ge(*banks.read_out(("in", name, c % 2)))
                if c < 4:
                    src, dst, wc = (lambda j: pad_kv[:, c, :, j:j + S]), conv_kv[:, c], 2 + c
                else:
                    src, dst, wc = (lambda j: pad_q[:, c - 4, j:j + S]), conv_q[:, c - 4], c - 4
                V.tensor_scalar(dst, src(0), cw[:, wc, 0:1], None, ALU.mult).then_inc(dve_step, 1)
                dve.wait_ge(dve_step, dve_steps())
                for j in range(1, CONV):
                    V.scalar_tensor_tensor(dst, src(j), cw[:, wc, j:j + 1], dst, ALU.mult, ALU.add).then_inc(dve_step, 1)
                    dve.wait_ge(dve_step, dve_steps())
                dve.sem_inc(conv_ready, 1)
            dve.wait_ge(*banks.full("ab"))
            o = banks.tile("ab")
            V.tensor_copy(ab, o[:, 0:64].rearrange("p (t n) -> p t n", t=4)).then_inc(banks.when_read("ab"), 1)
            dve.wait_ge(*banks.read_out("ab"))
            z, y, s, s2, q = (sp[:, i, :] for i in range(5))
            z3 = z.rearrange("p (t n) -> p t n", t=4)
            V.tensor_tensor(z3, ab[:, :, 0:8], M("dt_bias").unsqueeze(1).to_broadcast([P, 4, 8]), ALU.add).then_inc(dve_step, 1)
            dve.wait_ge(dve_step, dve_steps())
            V.tensor_scalar(y, z, -1.0, None, ALU.mult).then_inc(dve_step, 1)
            dve.wait_ge(dve_step, dve_steps())
            V.tensor_tensor(y, y, z, ALU.max).then_inc(dve_step, 1)
            dve.wait_ge(dve_step, dve_steps())
            dve.sem_inc(softplus_arg, 1)
            dve.wait_ge(softplus_exp, 1)
            log1p(V, dve, y, s, s2, q)
            V.tensor_scalar(z, z, 0.0, None, ALU.max).then_inc(dve_step, 1)
            dve.wait_ge(dve_step, dve_steps())
            V.tensor_tensor(z, z, q, ALU.add).then_inc(dve_step, 1)
            dve.wait_ge(dve_step, dve_steps())
            V.scalar_tensor_tensor(g_log.rearrange("p t d h -> p t (d h)"), z3, -1.0,
                                   sp[:, 5, 0:8].unsqueeze(1).to_broadcast([P, 4, 8]), ALU.mult, ALU.mult).then_inc(dve_step, 1)
            dve.wait_ge(dve_step, dve_steps())
            dve.sem_inc(g_ready, 1)
            b2 = beta.rearrange("p t d h -> p (t d h)")
            V.tensor_scalar(b2, b2, 1.0, None, ALU.add).then_inc(dve_step, 1)
            dve.wait_ge(dve_step, dve_steps())
            V.reciprocal(b2, b2).then_inc(dve_step, 1)
            dve.wait_ge(dve_step, dve_steps())
            V.tensor_tensor(nlam[:, 4:5], nlam[:, 3:4], nlam[:, 2:3], ALU.subtract).then_inc(dve_step, 1)
            dve.wait_ge(dve_step, dve_steps())
            V.tensor_scalar(nlam[:, 4:5], nlam[:, 4:5], -LAM_INIT, None, ALU.add).then_inc(dve_step, 1)
            dve.wait_ge(dve_step, dve_steps())
            for t in range(4):
                dve.wait_ge(*banks.read_out(("kv_tm", t)))
            dve.wait_ge(*banks.read_out("q_tm"))
            sq = scratch.rearrange("p (t n) -> p t n", t=4)
            V.tensor_tensor(sq, kv_tm[:, :, 0:GW], kv_tm[:, :, 0:GW], ALU.mult).then_inc(dve_step, 1)
            dve.wait_ge(dve_step, dve_steps())
            V.tensor_reduce(stat[:, 8:24], scratch.rearrange("p (g n) -> p g n", n=HD), AX.X, ALU.add).then_inc(dve_step, 1)
            dve.wait_ge(dve_step, dve_steps())
            V.tensor_tensor(scratch[:, 0:512], q_tm.rearrange("p t n -> p (t n)"), q_tm.rearrange("p t n -> p (t n)"), ALU.mult).then_inc(dve_step, 1)
            dve.wait_ge(dve_step, dve_steps())
            V.tensor_reduce(stat[:, 24:32], scratch[:, 0:512].rearrange("p (g n) -> p g n", n=HD), AX.X, ALU.add).then_inc(dve_step, 1)
            dve.wait_ge(dve_step, dve_steps())
            dve.sem_inc(kq_squares, 1)
            dve.wait_ge(kq_rstd, 1)
            for t in range(4):
                k4 = kv_tm[:, t, 0:GW].rearrange("p (h n) -> p h n", h=H)
                V.tensor_tensor(k4, k4, stat[:, 32 + 4 * t:36 + 4 * t].unsqueeze(2).to_broadcast([P, H, HD]), ALU.mult).then_inc(dve_step, 1)
                dve.wait_ge(dve_step, dve_steps())
            for t in range(NT):
                q4 = q_tm[:, t, :].rearrange("p (h n) -> p h n", h=H)
                V.tensor_tensor(q4, q4, stat[:, 48 + 4 * t:52 + 4 * t].unsqueeze(2).to_broadcast([P, H, HD]), ALU.mult).then_inc(dve_step, 1)
                dve.wait_ge(dve_step, dve_steps())
            q2 = q_tm.rearrange("p t n -> p (t n)")
            V.tensor_scalar(q2, q2, HD ** -0.5, None, ALU.mult).then_inc(dve_step, 1)
            dve.wait_ge(dve_step, dve_steps())
            dve.sem_inc(kq_normed, 1)
            dve.wait_ge(*banks.read_out("gc"))
            V.tensor_tensor(begc, egc, beta.rearrange("p t d h -> p d t h"), ALU.mult).then_inc(dve_step, 1)
            dve.wait_ge(dve_step, dve_steps())
            dve.sem_inc(begc_ready, 1)
            for name, buf in (("df_q", df_q), ("df_k", df_k)):
                for f in range(2):
                    dve.wait_ge(*banks.full(("rot", name, f)))
                    o = banks.tile(("rot", name, f))
                    t_ = buf[:, f, :] if name == "df_q" else buf[:, f, S:2 * S]
                    V.tensor_tensor(scratch[:, 0:S], o[:, 0:S], K("sin"), ALU.mult).then_inc(banks.when_read(("rot", name, f)), 1)
                    dve.wait_ge(*banks.read_out(("rot", name, f)))
                    V.tensor_tensor(t_, t_, K("cos"), ALU.mult).then_inc(dve_step, 1)
                    dve.wait_ge(dve_step, dve_steps())
                    V.tensor_tensor(t_, t_, scratch[:, 0:S], ALU.add).then_inc(dve_step, 1)
                    dve.wait_ge(dve_step, dve_steps())
                    dve.sem_inc(roped, 1)

            def attend(n):
                if n < NA_N:
                    kind = ATT[n][0]
                    c = 4 * (n % 4)
                    for m in range(1 if kind == "na" else 2):
                        dve.wait_ge(*banks.full(("s", n, m)))
                        o = banks.tile(("s", n, m))
                        if n >= 4 and m == 0:
                            dve.wait_ge(*banks.read_out(("pv", n - 4)))
                        V.tensor_reduce(smax[:, 0, c + m:c + m + 1], o, AX.X, ALU.max, negate=True).then_inc(dve_step, 1)
                        dve.wait_ge(dve_step, dve_steps())
                        if kind == "df":
                            V.tensor_scalar(smax[:, 0, c + m:c + m + 1], smax[:, 0, c + m:c + m + 1], 32 ** -0.5, None, ALU.mult).then_inc(dve_step, 1)
                            dve.wait_ge(dve_step, dve_steps())
                    dve.sem_inc(smax_ready, 1)
                    dve.wait_ge(prob_exp, n + 1)
                    w = 1 if kind == "na" else 2
                    V.reciprocal(smax[:, 2, c:c + w], smax[:, 1, c:c + w]).then_inc(dve_step, 1)
                    dve.wait_ge(dve_step, dve_steps())
                    if kind == "df":
                        if n >= 9:
                            dve.wait_ge(*banks.full(("pT", n - 1)))
                        V.tensor_tensor(smax[:, 3, c:c + 1], smax[:, 2, c + 1:c + 2], nlam[:, 4:5], ALU.mult).then_inc(dve_step, 1)
                        dve.wait_ge(dve_step, dve_steps())
                        V.tensor_scalar(prob[:, 0, :], prob[:, 0, :], smax[:, 2, c:c + 1], None, ALU.mult).then_inc(dve_step, 1)
                        dve.wait_ge(dve_step, dve_steps())
                        V.scalar_tensor_tensor(prob[:, 2, :], prob[:, 1, :], smax[:, 3, c:c + 1], prob[:, 0, :], ALU.mult, ALU.add).then_inc(dve_step, 1)
                        dve.wait_ge(dve_step, dve_steps())
                    dve.sem_inc(prob_ready, 1)
                if 1 <= n <= len(PAIRS):
                    mod_in(*PAIRS[n - 1])

            n = 0
            for t in range(4):
                dve.wait_ge(*banks.read_out(("kk", t)))
                for d in range(2):
                    g = G(t, d)
                    dve.wait_ge(*banks.full(("gb", t, d)))
                    o = banks.tile(("gb", t, d)).rearrange("p (h n) -> p h n", h=H)
                    gb = gcum[:, d, t, :].unsqueeze(2).to_broadcast([P, H, P])
                    V.tensor_tensor(dmat, o, gb, ALU.subtract).then_inc(dve_step, 1)
                    dve.wait_ge(dve_step, dve_steps())
                    V.tensor_copy(glast[:, d, t, :], o[:, :, (P - 1, 0)[d]]).then_inc(banks.when_read(("gb", t, d)), 1)
                    dve.wait_ge(*banks.read_out(("gb", t, d)))
                    V.tensor_tensor(ekd[:, d, t, :], glast[:, d, t, :], gcum[:, d, t, :], ALU.subtract).then_inc(dve_step, 1)
                    dve.wait_ge(dve_step, dve_steps())
                    if t >= 2:
                        V.tensor_scalar(etm, dmat, 0.0, None, ALU.min).then_inc(dve_step, 1)
                        dve.wait_ge(dve_step, dve_steps())
                    V.tensor_scalar(emat, dmat, 0.0, None, ALU.max).then_inc(dve_step, 1)
                    dve.wait_ge(dve_step, dve_steps())
                    dve.sem_inc(decay_arg, 1)
                    dve.wait_ge(decay_masked, g + 1)
                    low = solve[d][:, 0]
                    if t > 0:
                        dve.wait_ge(*banks.full(("uw", t - 1, d)))
                    V.tensor_tensor(low, kk_sb, emat, ALU.mult).then_inc(dve_step, 1)
                    dve.wait_ge(dve_step, dve_steps())
                    V.tensor_tensor(low, low, beta[:, t, d, :].unsqueeze(2).to_broadcast([P, H, P]), ALU.mult).then_inc(dve_step, 1)
                    dve.wait_ge(dve_step, dve_steps())
                    dve.sem_inc(lower_ready, 1)
                    if t >= 2:
                        dve.wait_ge(*banks.full(("qk", t)))
                        o = banks.tile(("qk", t)).rearrange("p (h n) -> p h n", h=H)
                        V.tensor_tensor(qk[:, d, t - 2], o, etm, ALU.mult).then_inc(dve_step, 1)
                        dve.wait_ge(dve_step, dve_steps())
                        if d == 1:
                            dve.sem_inc(banks.when_read(("qk", t)), 1)
                        dve.sem_inc(qk_ready, 1)
                attend(n)
                attend(n + 1)
                n += 2
                for lv in range(1, 7):
                    for d in range(2):
                        if lv == 1:
                            dve.wait_ge(inverse_begun, 2 * G(t, d) + 2)
                        dve.wait_ge(*banks.full(("x", t, d, lv)))
                        o = banks.tile(("x", t, d, lv)).rearrange("p (h n) -> p h n", h=H)
                        mask = K(("level_f", "level_b")[d])[:, P * lv:P * lv + P].unsqueeze(1).to_broadcast([P, H, P])
                        V.tensor_tensor(solve[d][:, 0], o, mask, ALU.mult).then_inc(banks.when_read(("x", t, d, lv)), 1)
                    if lv in FILL_LEVELS:
                        attend(n)
                        n += 1
                    for d in range(2):
                        for key, i in ((("dt", t, d, lv), 2), (("dtt", t, d, lv), 3)):
                            if key[0] == "dt" and lv == 6:
                                continue
                            if key[0] == "dt":
                                dve.wait_ge(*banks.full(("x", t, d, lv)))
                            dve.wait_ge(*banks.full(key))
                            o = banks.tile(key).rearrange("p (h n) -> p h n", h=H)
                            V.tensor_tensor(solve[d][:, i], solve[d][:, i], o, ALU.subtract).then_inc(banks.when_read(key), 1)
                            dve.wait_ge(*banks.read_out(key))
            for step, d, t in ORDER:
                dve.wait_ge(*banks.read_out(("uw", t, d)))
                u = uw[:, d, t, 0:GW].rearrange("p (h n) -> p h n", h=H)
                if step:
                    dve.wait_ge(*banks.full(("ws", step, d)))
                    o = banks.tile(("ws", step, d))
                    ins = V.tensor_tensor(vnew[:, d], u, o[:, 0:GW].rearrange("p (h n) -> p h n", h=H), ALU.subtract)
                else:
                    ins = V.tensor_copy(vnew[:, d], u)
                ins.then_inc(dve_step, 1)
                dve.wait_ge(dve_step, dve_steps())
                dve.sem_inc(vnew_ready[d], 1)
                if step:
                    if t >= 2:
                        e4 = egc[:, d, t, :].unsqueeze(2).to_broadcast([P, H, HD])
                        o4 = o[:, GW:2 * GW].rearrange("p (h n) -> p h n", h=H)
                        if t == 2 + d:
                            V.tensor_tensor(o_acc[:, t - 2], o4, e4, ALU.mult).then_inc(dve_step, 1)
                            dve.wait_ge(dve_step, dve_steps())
                        else:
                            s4 = scratch[:, 0:GW].rearrange("p (h n) -> p h n", h=H)
                            V.tensor_tensor(s4, o4, e4, ALU.mult).then_inc(dve_step, 1)
                            dve.wait_ge(dve_step, dve_steps())
                            V.tensor_tensor(o_acc[:, t - 2], o_acc[:, t - 2], s4, ALU.add).then_inc(dve_step, 1)
                            dve.wait_ge(dve_step, dve_steps())
                    dve.sem_inc(banks.when_read(("ws", step, d)), 1)
                dve.wait_ge(*banks.full(("so", step, d)))
                o = banks.tile(("so", step, d))
                if step < 3:
                    dve.wait_ge(gls_ready, G(t, d) + 1)
                    for g in range(2):
                        if step == 0:
                            V.tensor_copy(state[:, d, g, :], o[:, HD * g:HD * g + HD]).then_inc(dve_step, 1)
                            dve.wait_ge(dve_step, dve_steps())
                        else:
                            V.scalar_tensor_tensor(state[:, d, g, :], state[:, d, g, :], gls[:, d, t, g:g + 1],
                                                   o[:, HD * g:HD * g + HD], ALU.mult, ALU.add).then_inc(dve_step, 1)
                            dve.wait_ge(dve_step, dve_steps())
                    dve.sem_inc(state_ready[d], 1)
                if t >= 2:
                    V.tensor_tensor(o_acc[:, t - 2], o_acc[:, t - 2], o[:, GW:2 * GW].rearrange("p (h n) -> p h n", h=H), ALU.add).then_inc(dve_step, 1)
                    dve.wait_ge(dve_step, dve_steps())
                dve.sem_inc(banks.when_read(("so", step, d)), 1)
                if d == 1:
                    attend(n)
                    n += 1
            for n in range(NA_N - 2, NA_N):
                dve.wait_ge(*banks.read_out(("pv", n)))
            o8 = o_acc.rearrange("p t h n -> p (t h) n")
            s8 = scratch[:, 0:512].rearrange("p (g n) -> p g n", n=HD)
            V.tensor_tensor(s8, o8, o8, ALU.mult).then_inc(dve_step, 1)
            dve.wait_ge(dve_step, dve_steps())
            V.tensor_reduce(stat[:, 8:16], s8, AX.X, ALU.add).then_inc(dve_step, 1)
            dve.wait_ge(dve_step, dve_steps())
            s9 = scratch[:, 512:1024].rearrange("p (t n) -> p t n", t=NT)
            V.tensor_tensor(s9, mix[:, :, 512:768], mix[:, :, 512:768], ALU.mult).then_inc(dve_step, 1)
            dve.wait_ge(dve_step, dve_steps())
            V.tensor_reduce(stat[:, 16:24], scratch[:, 512:1024].rearrange("p (g n) -> p g n", n=HD), AX.X, ALU.add).then_inc(dve_step, 1)
            dve.wait_ge(dve_step, dve_steps())
            dve.sem_inc(head_squares, 1)
            dve.wait_ge(head_rstd, 1)
            for t in range(NT):
                dn4 = mix[:, t, 256:512].rearrange("p (h n) -> p h n", h=H)
                df4 = mix[:, t, 512:768].rearrange("p (h n) -> p h n", h=H)
                for dst, src, c, gain in ((dn4, o_acc[:, t], 32, "dn_norm"), (df4, df4, 40, "df_norm")):
                    V.tensor_tensor(dst, src, stat[:, c + 4 * t:c + 4 * t + 4].unsqueeze(2).to_broadcast([P, H, HD]), ALU.mult).then_inc(dve_step, 1)
                    dve.wait_ge(dve_step, dve_steps())
                    V.tensor_tensor(dst, dst, M(gain).unsqueeze(1).to_broadcast([P, H, HD]), ALU.mult).then_inc(dve_step, 1)
                    dve.wait_ge(dve_step, dve_steps())
                V.tensor_tensor(mix[:, t, 256:512], mix[:, t, 256:512], gate_tm[:, t, :], ALU.mult).then_inc(dve_step, 1)
                dve.wait_ge(dve_step, dve_steps())
                V.tensor_scalar(mix[:, t, 512:768], mix[:, t, 512:768], 1.0 - LAM_INIT, None, ALU.mult).then_inc(dve_step, 1)
                dve.wait_ge(dve_step, dve_steps())
            dve.sem_inc(mix_ready, 3)
            dve.sem_inc(mixers_done, 1)

            def row_in(tag, b, diag=diag):
                v = ROW_OF[tag.removeprefix("b_")]
                for g in range(2):
                    n = 2 * ROWS.index(tag) + g
                    if n:
                        dve.wait_ge(*banks.full(("row", ROWS[(n - 1) // 2], (n - 1) % 2)))
                    V.tensor_tensor(diag, ident.unsqueeze(1).to_broadcast([P, 4, P]),
                                    mfm[:, b, KT * v + 4 * g:KT * v + 4 * g + 4, 0].unsqueeze(2).to_broadcast([P, 4, P]), ALU.mult).then_inc(dve_step, 1)
                    dve.wait_ge(dve_step, dve_steps())
                    dve.sem_inc(diag_ready, 1)

            row_in("gate1", 0)
            for g in range(2):
                dve.wait_ge(*banks.read_out(("row", "gate1", g)))
            for c in range(4):
                for t in range(NT):
                    dve.wait_ge(*banks.full(("wo", c, t)))
                    o = banks.tile(("wo", c, t))
                    cs = slice(256 * c, 256 * c + 256)
                    tmp = acc[:, 1, 0:256]
                    V.tensor_tensor(tmp, o[:, 0:256], rows[:, 0, cs], ALU.mult).then_inc(banks.when_read(("wo", c, t)), 1)
                    dve.wait_ge(*banks.read_out(("wo", c, t)))
                    V.tensor_tensor(x[:, t, cs], x[:, t, cs], tmp, ALU.add).then_inc(dve_step, 1)
                    dve.wait_ge(dve_step, dve_steps())
            dve.sem_inc(x1_ready, 2)
            for tag in ("scale2", "shift2", "gate2"):
                row_in(tag, 0)
            for g in range(2):
                dve.wait_ge(*banks.read_out(("row", "scale2", g)))
                dve.wait_ge(*banks.read_out(("row", "shift2", g)))
            dve.wait_ge(gain_loaded, 16)
            V.scalar_tensor_tensor(rows[:, 1, :], rows[:, 1, :], 1.0, acc[:, 0, :], ALU.add, ALU.mult).then_inc(dve_step, 1)
            dve.wait_ge(dve_step, dve_steps())
            dve.wait_ge(rstd_ready, 2)
            for t in range(NT):
                V.tensor_scalar(h2[:, t, :], x[:, t, :], rstat[:, 2 + t:3 + t], None, ALU.mult).then_inc(dve_step, 1)
                dve.wait_ge(dve_step, dve_steps())
                V.tensor_tensor(h2[:, t, :], h2[:, t, :], rows[:, 1, :], ALU.mult).then_inc(dve_step, 1)
                dve.wait_ge(dve_step, dve_steps())
                V.tensor_tensor(h2[:, t, :], h2[:, t, :], rows[:, 2, :], ALU.add).then_inc(dve_step, 1)
                dve.wait_ge(dve_step, dve_steps())
                dve.sem_inc(h2_ready, 1)
            V.memset(acc, 0.0).then_inc(dve_step, 1)
            dve.wait_ge(dve_step, dve_steps())
            dve.wait_ge(*banks.full("rt"))
            o = banks.tile("rt")
            for t in range(NT):
                V.tensor_reduce(rstat[:, 4 + t:5 + t], o[:, E1 * t:E1 * t + E1], AX.X, ALU.max, negate=True).then_inc(dve_step, 1)
                dve.wait_ge(dve_step, dve_steps())
            dve.sem_inc(rt_max, 2)
            dve.wait_ge(rt_exp, 1)
            V.reciprocal(rstat[:, 8:10], rstat[:, 6:8]).then_inc(dve_step, 1)
            dve.wait_ge(dve_step, dve_steps())
            for t in range(NT):
                V.tensor_scalar(rt[:, t, :], rt[:, t, :], rstat[:, 8 + t:9 + t], None, ALU.mult).then_inc(dve_step, 1)
                dve.wait_ge(dve_step, dve_steps())
            dve.sem_inc(aff_ready, 1)
            dve.wait_ge(*banks.full("affT"))
            o = banks.tile("affT")
            work, a0, tmp, pos, gat = (aff[0:E1, i, :] for i in range(5))
            V.tensor_copy(work, o[0:E1, 0:S]).then_inc(dve_step, 1)
            dve.wait_ge(dve_step, dve_steps())
            V.tensor_copy(a0, o[0:E1, 0:S]).then_inc(banks.when_read("affT"), 1)
            dve.wait_ge(*banks.read_out("affT"))
            for r in range(CAP1 // 8):
                V.max(top8[0:E1, :], work).then_inc(dve_step, 1)
                dve.wait_ge(dve_step, dve_steps())
                V.match_replace(work, top8[0:E1, :], work, -1.0).then_inc(dve_step, 1)
                dve.wait_ge(dve_step, dve_steps())
            V.tensor_scalar(tmp, work, -1.0, None, ALU.is_equal).then_inc(dve_step, 1)
            dve.wait_ge(dve_step, dve_steps())
            V.tensor_tensor(gat, a0, tmp, ALU.mult).then_inc(dve_step, 1)
            dve.wait_ge(dve_step, dve_steps())
            V.memset(a0, 1.0).then_inc(dve_step, 1)
            dve.wait_ge(dve_step, dve_steps())
            V.tensor_tensor_scan(pos, a0, tmp, 0.0, ALU.mult, ALU.add).then_inc(dve_step, 1)
            dve.wait_ge(dve_step, dve_steps())
            V.tensor_tensor(pos, pos, tmp, ALU.mult).then_inc(dve_step, 1)
            dve.wait_ge(dve_step, dve_steps())
            V.tensor_scalar(pos, pos, -1.0, None, ALU.add).then_inc(dve_step, 1)
            dve.wait_ge(dve_step, dve_steps())
            dve.sem_inc(choice_ready, 2)
            dve.wait_ge(*banks.full("pgT"))
            o = banks.tile("pgT")
            V.tensor_copy(pg_tm, o[:, 0:64].rearrange("p (i t e) -> p i t e", i=2, t=NT)).then_inc(banks.when_read("pgT"), 1)
            dve.wait_ge(*banks.read_out("pgT"))
            dve.sem_inc(m_hid, 1)
            dve.sem_inc(m_acc, 1)
            with dve.Fori(0, E1) as e:
                moe1_vector(dve, e)
            for t in range(NT):
                dve.wait_ge(m_acc, 2 * E1 + 1)
                for g in range(2):
                    dve.wait_ge(*banks.read_out(("row", "gate2", g)))
                V.tensor_tensor(acc[:, t, :], acc[:, t, :], rows[:, 0, :], ALU.mult).then_inc(dve_step, 1)
                dve.wait_ge(dve_step, dve_steps())
                V.tensor_tensor(x[:, t, :], x[:, t, :], acc[:, t, :], ALU.add).then_inc(dve_step, 1)
                dve.wait_ge(dve_step, dve_steps())
                dve.sem_inc(x2_ready, 1)
            dve.wait_ge(rstd_ready, 3)
            dve.wait_ge(gain_loaded, 32)
            for t in range(NT):
                V.scalar_tensor_tensor(x[:, t, :], x[:, t, :], rstat[:, 12 + t:13 + t], rows[:, 1, :], ALU.mult, ALU.mult).then_inc(dve_step, 1)
                dve.wait_ge(dve_step, dve_steps())
            dve.sem_inc(block1_ready, 1)
            V.scalar_tensor_tensor(scale2, mfm[:, 1, KT:2 * KT, 0], 1.0, M("norm1_2"), ALU.add, ALU.mult).then_inc(dve_step, 1)
            dve.wait_ge(dve_step, dve_steps())
            dve.wait_ge(rstd_ready, 4)
            for t in range(NT):
                V.tensor_scalar(xn2[:, t, :], x[:, t, :], stat2[:, 2 + t:3 + t], None, ALU.mult).then_inc(dve_step, 1)
                dve.wait_ge(dve_step, dve_steps())
                dve.sem_inc(xn2_ready, 1)
            V.memset(xr[:, :, 0:LEAD], 0.0).then_inc(dve_step, 1)
            dve.wait_ge(dve_step, dve_steps())
            dve.sem_inc(xr_zero, 1)
            for kk in range(4):
                dve.wait_ge(*banks.full(("uT", kk)))
                o = banks.tile(("uT", kk))
                for c in range(2):
                    k = 2 * kk + c
                    V.tensor_scalar(uT[:, k, :], o[:, S * c:S * c + S], scale2[:, k:k + 1], mfm[:, 1, k, 0:1], ALU.mult, ALU.add).then_inc(dve_step, 1)
                    dve.wait_ge(dve_step, dve_steps())
                dve.sem_inc(banks.when_read(("uT", kk)), 1)
            z, y, s, s2, q = (nsp[:, i, :] for i in range(5))
            V.tensor_scalar(z, M("lru"), -1.0, None, ALU.mult).then_inc(dve_step, 1)
            dve.wait_ge(dve_step, dve_steps())
            V.tensor_tensor(y, z, M("lru"), ALU.max).then_inc(dve_step, 1)
            dve.wait_ge(dve_step, dve_steps())
            dve.sem_inc(lru_arg, 1)
            dve.wait_ge(lru_exp, 1)
            log1p(V, dve, y, s, s2, q)
            V.tensor_scalar(z, z, 0.0, None, ALU.max).then_inc(dve_step, 1)
            dve.wait_ge(dve_step, dve_steps())
            V.tensor_tensor(z, z, q, ALU.add).then_inc(dve_step, 1)
            dve.wait_ge(dve_step, dve_steps())
            V.tensor_scalar(cl, z, -8.0, None, ALU.mult).then_inc(dve_step, 1)
            dve.wait_ge(dve_step, dve_steps())
            dve.wait_ge(rstd_ready, 5)
            for t in range(NT):
                V.scalar_tensor_tensor(ckv[:, t, :], ckv[:, t, :], stat2[:, 6 + t:7 + t], M("kv_norm"), ALU.mult, ALU.mult).then_inc(dve_step, 1)
                dve.wait_ge(dve_step, dve_steps())
            dve.sem_inc(ckv_normed, 1)
            for n, (t, par, pr) in enumerate(IDXB):
                dve.wait_ge(*banks.read_out(("idx", t, par, pr)))
                if n == 0:
                    dve.wait_ge(*banks.read_out("ki"))
                for m in range(2):
                    h = 4 * pr + 2 * m + par
                    if par == 0 and pr == 0 and m == 0:
                        V.tensor_scalar(score[:, t, :], relu[:, m, :], wi[:, t, h:h + 1], None, ALU.mult).then_inc(dve_step, 1)
                        dve.wait_ge(dve_step, dve_steps())
                    else:
                        V.scalar_tensor_tensor(score[:, t, :], relu[:, m, :], wi[:, t, h:h + 1], score[:, t, :], ALU.mult, ALU.add).then_inc(dve_step, 1)
                        dve.wait_ge(dve_step, dve_steps())
                dve.sem_inc(relu_used, 1)
            causal = K2("causal").rearrange("p (t s) -> p t s", t=NT)
            dve.wait_ge(const2_loaded, 16)
            V.scalar_tensor_tensor(work2, score, IDX_SCALE, causal, ALU.mult, ALU.add).then_inc(dve_step, 1)
            dve.wait_ge(dve_step, dve_steps())

            def top_round(r):
                for t in range(NT):
                    V.max(top2[:, t, :], work2[:, t, :]).then_inc(dve_step, 1)
                    dve.wait_ge(dve_step, dve_steps())
                    V.match_replace(work2[:, t, :], top2[:, t, :], work2[:, t, :], -3e38).then_inc(dve_step, 1)
                    dve.wait_ge(dve_step, dve_steps())

            cw = M("conv_2").rearrange("p (c j) -> p c j", j=CONV2)
            for r in range(TOPK // 8):
                top_round(r)
            mask = chosen.rearrange("p (t s) -> p t s", t=NT)
            V.tensor_scalar(mask, work2, -3e38, None, ALU.is_equal).then_inc(dve_step, 1)
            dve.wait_ge(dve_step, dve_steps())
            V.tensor_scalar(mask, mask, -1.0, -NEG, ALU.add, ALU.mult).then_inc(dve_step, 1)
            dve.wait_ge(dve_step, dve_steps())
            V.tensor_tensor(mask, mask, causal, ALU.add).then_inc(dve_step, 1)
            dve.wait_ge(dve_step, dve_steps())
            dve.sem_inc(chosen_ready, 1)
            for n in range(RT):
                dve.wait_ge(*banks.read_out(("in2", FIRST2["xr"] + n // 2)))
                V.tensor_scalar(xc[:, n, :], xr[:, n, 0:S], cw[:, n, 0:1], M("conv_b_2")[:, n:n + 1], ALU.mult, ALU.add).then_inc(dve_step, 1)
                dve.wait_ge(dve_step, dve_steps())
                for j in range(1, CONV2):
                    V.scalar_tensor_tensor(xc[:, n, :], xr[:, n, j:j + S], cw[:, n, j:j + 1], xc[:, n, :], ALU.mult, ALU.add).then_inc(dve_step, 1)
                    dve.wait_ge(dve_step, dve_steps())
                dve.sem_inc(xc_ready, 1)
            for n in range(RT):
                dve.wait_ge(rg_ready, n + 1)
                V.tensor_tensor(xc[:, n, :], xc[:, n, :], th[:, n, :], ALU.mult).then_inc(dve_step, 1)
                dve.wait_ge(dve_step, dve_steps())
                V.tensor_scalar(la[:, n, :], rb[:, n, :], cl[:, n:n + 1], None, ALU.mult).then_inc(dve_step, 1)
                dve.wait_ge(dve_step, dve_steps())
            dve.sem_inc(la_ready, 1)
            flat = lambda v: v.rearrange("p c t -> p (c t)")
            for n in range(AH):
                dve.wait_ge(*banks.full(("l2", n)))
                o = banks.tile(("l2", n))
                dve.wait_ge(hbias_ready, n + 1)
                if n >= 2:
                    dve.wait_ge(*banks.full(("p2T", n - 2)))
                c = 3 * (n % 4)
                V.scalar_tensor_tensor(prob2[:, n % 2].rearrange("p t s -> p (t s)"), o, ATT_SCALE, hbias[n % 2],
                                       ALU.mult, ALU.add).then_inc(banks.when_read(("l2", n)), 1)
                dve.wait_ge(*banks.read_out(("l2", n)))
                dve.sem_inc(hbias_used, 1)
                V.tensor_reduce(smax2[:, c, :], prob2[:, n % 2], AX.X, ALU.max, negate=True).then_inc(dve_step, 1)
                dve.wait_ge(dve_step, dve_steps())
                dve.sem_inc(smax2_ready, 1)
                dve.wait_ge(exp2_ready, n + 1)
                V.reciprocal(smax2[:, c + 2, :], smax2[:, c + 1, :]).then_inc(dve_step, 1)
                dve.wait_ge(dve_step, dve_steps())
                for t in range(NT):
                    V.tensor_scalar(prob2[:, n % 2, t, :], prob2[:, n % 2, t, :], smax2[:, c + 2, t:t + 1], None, ALU.mult).then_inc(dve_step, 1)
                    dve.wait_ge(dve_step, dve_steps())
                dve.sem_inc(prob2_ready, 1)
                if n == 1:
                    dve.wait_ge(decay2_ready, 1)
                    V.tensor_tensor(flat(rb), flat(la), flat(la), ALU.mult).then_inc(dve_step, 1)
                    dve.wait_ge(dve_step, dve_steps())
                    V.scalar_tensor_tensor(flat(rb), flat(rb), 1.0, flat(th), ALU.add, ALU.mult).then_inc(dve_step, 1)
                    dve.wait_ge(dve_step, dve_steps())
                    V.tensor_scalar(flat(th), flat(rb), -1.0, None, ALU.mult).then_inc(dve_step, 1)
                    dve.wait_ge(dve_step, dve_steps())
                    dve.sem_inc(lru_var, 1)
                if n == 3:
                    dve.wait_ge(lru_std, 1)
                    V.tensor_tensor(flat(xc), flat(xc), flat(th), ALU.mult).then_inc(dve_step, 1)
                    dve.wait_ge(dve_step, dve_steps())
                if n >= 4:
                    for m in range(3 * (n - 4), min(3 * (n - 3), RT)):
                        V.tensor_tensor_scan(rb[:, m, :], la[:, m, :], xc[:, m, :], 0.0, ALU.mult, ALU.add).then_inc(dve_step, 1)
                        dve.wait_ge(dve_step, dve_steps())
                        if m % 2 == 0:
                            dve.wait_ge(*banks.read_out(("in2", FIRST2["gr"] + m // 2)))
                        V.tensor_tensor(gr[:, m, :], gr[:, m, :], rb[:, m, :], ALU.mult).then_inc(dve_step, 1)
                        dve.wait_ge(dve_step, dve_steps())
                        dve.sem_inc(gh_ready, 1)
            for c in range(KT // 2):
                dve.wait_ge(*banks.full(("ya", c)))
                o = banks.tile(("ya", c))
                dve.wait_ge(mg_ready, 2 * c + 2)
                mm_ = mixT2[:, 2 * c:2 * c + 2, :]
                V.tensor_tensor(mm_, o.rearrange("p (c t) -> p c t", c=2), mg[:, 2 * c:2 * c + 2, :], ALU.mult).then_inc(banks.when_read(("ya", c)), 1)
                dve.wait_ge(*banks.read_out(("ya", c)))
            for c in range(KT // 2):
                dve.wait_ge(*banks.full(("yb", c)))
                o = banks.tile(("yb", c))
                dve.wait_ge(mg_ready, KT + 2 * c + 2)
                g_ = mg[:, KT + 2 * c:KT + 2 * c + 2, :]
                V.tensor_tensor(g_, o.rearrange("p (c t) -> p c t", c=2), g_, ALU.mult).then_inc(banks.when_read(("yb", c)), 1)
                dve.wait_ge(*banks.read_out(("yb", c)))
                V.tensor_tensor(mixT2[:, 2 * c:2 * c + 2, :], mixT2[:, 2 * c:2 * c + 2, :], g_, ALU.add).then_inc(dve_step, 1)
                dve.wait_ge(dve_step, dve_steps())
                dve.sem_inc(mix2_ready, 1)
            row_in("b_gate1", 1, diag2)
            for g in range(2):
                dve.wait_ge(*banks.read_out(("row", "b_gate1", g)))
            for c in range(4):
                dve.wait_ge(*banks.full(("wo2", c)))
                o = banks.tile(("wo2", c))
                cs = slice(256 * c, 256 * c + 256)
                tmp = acc2[:, 1, 0:512].rearrange("p (t n) -> p t n", t=NT)
                V.tensor_tensor(tmp, o.rearrange("p (t n) -> p t n", t=NT),
                                rows2[:, 0, cs].unsqueeze(1).to_broadcast([P, NT, 256]), ALU.mult).then_inc(banks.when_read(("wo2", c)), 1)
                dve.wait_ge(*banks.read_out(("wo2", c)))
                V.tensor_tensor(x[:, :, cs], x[:, :, cs], tmp, ALU.add).then_inc(dve_step, 1)
                dve.wait_ge(dve_step, dve_steps())
            dve.sem_inc(x3_ready, 1)
            dve.sem_inc(mixers2_done, 1)
            for tag in ("b_scale2", "b_shift2", "b_gate2"):
                row_in(tag, 1, diag2)
            for g in range(2):
                dve.wait_ge(*banks.read_out(("row", "b_scale2", g)))
                dve.wait_ge(*banks.read_out(("row", "b_shift2", g)))
            dve.wait_ge(gain2_loaded, 16)
            V.scalar_tensor_tensor(rows2[:, 1, :], rows2[:, 1, :], 1.0, acc2[:, 0, :], ALU.add, ALU.mult).then_inc(dve_step, 1)
            dve.wait_ge(dve_step, dve_steps())
            dve.wait_ge(rstd_ready, 6)
            for t in range(NT):
                V.tensor_scalar(u2[:, t, :], x[:, t, :], rs2[:, 2 + t:3 + t], None, ALU.mult).then_inc(dve_step, 1)
                dve.wait_ge(dve_step, dve_steps())
                V.tensor_tensor(u2[:, t, :], u2[:, t, :], rows2[:, 1, :], ALU.mult).then_inc(dve_step, 1)
                dve.wait_ge(dve_step, dve_steps())
                V.tensor_tensor(u2[:, t, :], u2[:, t, :], rows2[:, 2, :], ALU.add).then_inc(dve_step, 1)
                dve.wait_ge(dve_step, dve_steps())
                dve.sem_inc(u2_ready, 1)
            V.memset(acc2, 0.0).then_inc(dve_step, 1)
            dve.wait_ge(dve_step, dve_steps())
            NE = NG2 + E2
            dve.wait_ge(*banks.full("rt2"))
            o = banks.tile("rt2")
            V.tensor_tensor(lg, o[:, 0:NT * NE].rearrange("p (t e) -> p t e", t=NT),
                            M("router_b").unsqueeze(1).to_broadcast([P, NT, NE]), ALU.add).then_inc(banks.when_read("rt2"), 1)
            dve.wait_ge(*banks.read_out("rt2"))
            for t in range(NT):
                g4, e32 = lg[:, t, 0:NG2], lg[:, t, NG2:NE]
                gmax, a4 = rs2[:, 6 + t:7 + t], rt2[:, 4, t, 0:NG2]
                V.tensor_reduce(gmax, g4, AX.X, ALU.max).then_inc(dve_step, 1)
                dve.wait_ge(dve_step, dve_steps())
                V.tensor_scalar(rs2[:, 8 + t:9 + t], gmax, -1.0, None, ALU.mult).then_inc(dve_step, 1)
                dve.wait_ge(dve_step, dve_steps())
                V.tensor_scalar(a4, g4, gmax, None, ALU.is_equal).then_inc(dve_step, 1)
                dve.wait_ge(dve_step, dve_steps())
                V.scalar_tensor_tensor(a4, K2("group_no"), -float(NG2), a4, ALU.add, ALU.mult).then_inc(dve_step, 1)
                dve.wait_ge(dve_step, dve_steps())
                V.tensor_reduce(rs2[:, 16 + t:17 + t], a4, AX.X, ALU.min).then_inc(dve_step, 1)
                dve.wait_ge(dve_step, dve_steps())
                V.tensor_scalar(rs2[:, 16 + t:17 + t], rs2[:, 16 + t:17 + t], float(NG2), None, ALU.add).then_inc(dve_step, 1)
                dve.wait_ge(dve_step, dve_steps())
                em = rt2[:, 5, t, :]
                V.tensor_scalar(em, K2("expert_no"), rs2[:, 16 + t:17 + t], None, ALU.is_equal).then_inc(dve_step, 1)
                dve.wait_ge(dve_step, dve_steps())
                V.tensor_scalar(em, em, -1.0, -NEG, ALU.add, ALU.mult).then_inc(dve_step, 1)
                dve.wait_ge(dve_step, dve_steps())
                V.tensor_tensor(em, em, e32, ALU.add).then_inc(dve_step, 1)
                dve.wait_ge(dve_step, dve_steps())
                V.max(top8b[:, t, :], em).then_inc(dve_step, 1)
                dve.wait_ge(dve_step, dve_steps())
                V.max_index(idx8[:, t, :], top8b[:, t, :], em).then_inc(dve_step, 1)
                dve.wait_ge(dve_step, dve_steps())
                V.tensor_tensor(rs2[:, 12 + t:13 + t], top8b[:, t, 1:2], top8b[:, t, 0:1], ALU.subtract).then_inc(dve_step, 1)
                dve.wait_ge(dve_step, dve_steps())
                V.tensor_copy(rs2[:, 24 + 2 * t:26 + 2 * t], idx8[:, t, 0:2]).then_inc(dve_step, 1)
                dve.wait_ge(dve_step, dve_steps())
            dve.sem_inc(group_max, 1)
            for t in range(NT):
                V.tensor_scalar(rt2[:, 6, t, :], K("slot")[:, 0:E2], rs2[:, 24 + 2 * t:25 + 2 * t], None, ALU.is_equal).then_inc(dve_step, 1)
                dve.wait_ge(dve_step, dve_steps())
                V.tensor_scalar(rt2[:, 7, t, :], K("slot")[:, 0:E2], rs2[:, 25 + 2 * t:26 + 2 * t], None, ALU.is_equal).then_inc(dve_step, 1)
                dve.wait_ge(dve_step, dve_steps())
                V.tensor_tensor(masks[:, t, :], rt2[:, 6, t, :], rt2[:, 7, t, :], ALU.add).then_inc(dve_step, 1)
                dve.wait_ge(dve_step, dve_steps())
            dve.sem_inc(masks_ready, 1)
            dve.wait_ge(route_exp, 1)
            V.tensor_scalar(rs2[:, 30:32], rs2[:, 14:16], 1.0, None, ALU.add).then_inc(dve_step, 1)
            dve.wait_ge(dve_step, dve_steps())
            V.tensor_tensor(rs2[:, 30:32], rs2[:, 30:32], rs2[:, 10:12], ALU.mult).then_inc(dve_step, 1)
            dve.wait_ge(dve_step, dve_steps())
            V.reciprocal(rs2[:, 32:34], rs2[:, 30:32]).then_inc(dve_step, 1)
            dve.wait_ge(dve_step, dve_steps())
            V.tensor_tensor(rs2[:, 34:36], rs2[:, 32:34], rs2[:, 14:16], ALU.mult).then_inc(dve_step, 1)
            dve.wait_ge(dve_step, dve_steps())
            for t in range(NT):
                V.tensor_scalar(gates2[:, t, :], rt2[:, 6, t, :], rs2[:, 32 + t:33 + t], None, ALU.mult).then_inc(dve_step, 1)
                dve.wait_ge(dve_step, dve_steps())
                V.scalar_tensor_tensor(gates2[:, t, :], rt2[:, 7, t, :], rs2[:, 34 + t:35 + t], gates2[:, t, :], ALU.mult, ALU.add).then_inc(dve_step, 1)
                dve.wait_ge(dve_step, dve_steps())
            dve.wait_ge(*banks.full("pos2"))
            o = banks.tile("pos2")
            V.tensor_tensor(pos2, o[:, 0:2 * E2].rearrange("p (t e) -> p t e", t=NT), masks, ALU.mult).then_inc(dve_step, 1)
            dve.wait_ge(dve_step, dve_steps())
            V.tensor_scalar(pos2, pos2, -1.0, None, ALU.add).then_inc(dve_step, 1)
            dve.wait_ge(dve_step, dve_steps())
            V.tensor_reduce(rs2[:, 36:37], o[:, 2 * E2:3 * E2], AX.X, ALU.max).then_inc(dve_step, 1)
            dve.wait_ge(dve_step, dve_steps())
            dve.sem_inc(banks.when_read("pos2"), 1)
            V.tensor_copy(flag, rs2[:, 36:37]).then_inc(dve_step, 1)
            dve.wait_ge(dve_step, dve_steps())
            dve.sem_inc(flag_ready, 1)
            dve.sem_inc(n_hid, 1)
            dve.sem_inc(n_acc, 1)
            for b in range(8):
                dve.wait_ge(*banks.last(b))
            onehot_2(dve, 0, 0)
            pair2_vector(dve, 0, 0, first=True)
            with dve.Fori(1, E2 // 2 - 1) as j:
                pair2_vector(dve, 0, j)
            pair2_vector(dve, 0, E2 // 2 - 1, final=True)
            add2(dve, E2 - 1)
            more = dve.value_load(flag[0:1, 0:1], min_val=0, max_val=S)
            with dve.If(more > CAP2):
                with dve.Fori(1, PASSES2) as p:
                    dve.wait_ge(n_gathered, 32 * p + 1)
                    V.tensor_scalar(pos2, pos2, -float(CAP2), None, ALU.add).then_inc(pass_begun, 1)
                    dve.wait_ge(pass_begun, p)
                    onehot_2(dve, 32 * p, 0)
                    pair2_vector(dve, p, 0, first=True)
                    with dve.Fori(1, E2 // 2 - 1) as j:
                        pair2_vector(dve, p, j)
                    pair2_vector(dve, p, E2 // 2 - 1, final=True)
                    add2(dve, 32 * p + (E2 - 1))
            for g in range(2):
                dve.wait_ge(*banks.read_out(("row", "b_gate2", g)))
            for t in range(NT):
                V.tensor_tensor(acc2[:, t, :], acc2[:, t, :], rows2[:, 0, :], ALU.mult).then_inc(dve_step, 1)
                dve.wait_ge(dve_step, dve_steps())
                V.tensor_tensor(x[:, t, :], x[:, t, :], acc2[:, t, :], ALU.add).then_inc(dve_step, 1)
                dve.wait_ge(dve_step, dve_steps())
                dve.sem_inc(x4_ready, 1)
            dve.wait_ge(rstd_ready, 7)
            dve.wait_ge(gain2_loaded, 32)
            for t in range(NT):
                V.scalar_tensor_tensor(x[:, t, :], x[:, t, :], rs2[:, 22 + t:23 + t], rows2[:, 1, :], ALU.mult, ALU.mult).then_inc(dve_step, 1)
                dve.wait_ge(dve_step, dve_steps())
            dve.sem_inc(out_ready, 1)

        @block.gpsimd
        def _(pool):
            V = nc.gpsimd
            def rsqrt(dst, src, n, scale, eps):
                V.tensor_scalar(dst, src, scale, eps, ALU.mult, ALU.add).then_inc(pool_step, 1)
                pool.wait_ge(pool_step, pool_steps())
                V.tensor_tensor(dst, dst, half.to_broadcast([P, n]), ALU.pow).then_inc(pool_step, 1)
                pool.wait_ge(pool_step, pool_steps())

            pool.wait_ge(half_ready, 1)
            pool.wait_ge(squares_ready, 1)
            rsqrt(stat[:, 4:8], stat[:, 0:4], 4, 1.0 / D, EPS)
            pool.sem_inc(rstd_ready, 1)
            pool.wait_ge(na_bias_loaded, 16)
            nb = na_bias.rearrange("p i (r c) -> p (i r) c", c=GRID)
            V.tensor_tensor(nb, nb, K("window").unsqueeze(1).to_broadcast([P, 32, GRID]), ALU.add).then_inc(pool_step, 1)
            pool.wait_ge(pool_step, pool_steps())
            pool.sem_inc(na_bias_ready, 1)
            pool.wait_ge(kq_squares, 1)
            rsqrt(stat[:, 32:56], stat[:, 8:32], 24, 1.0, 1e-6)
            pool.sem_inc(kq_rstd, 1)
            pool.wait_ge(begc_ready, 1)
            for t in range(4):
                for d in range(2):
                    g = G(t, d)
                    pool.wait_ge(decay_exp, g + 1)
                    if t >= 2:
                        V.tensor_tensor(etm, etm, K(("tri_f", "tri_b")[d]).unsqueeze(1).to_broadcast([P, H, P]), ALU.mult).then_inc(pool_step, 1)
                        pool.wait_ge(pool_step, pool_steps())
                    V.tensor_tensor(emat, emat, K(("strict_f", "strict_b")[d]).unsqueeze(1).to_broadcast([P, H, P]), ALU.mult).then_inc(pool_step, 1)
                    pool.wait_ge(pool_step, pool_steps())
                    pool.sem_inc(decay_masked, 1)
                for d in range(2):
                    g = G(t, d)
                    pool.wait_ge(lower_ready, g + 1)
                    lf = (K("level_f")[:, 0:P], K("level_b")[:, 0:P])
                    id4 = ident.unsqueeze(1).to_broadcast([P, H, P])
                    V.tensor_tensor(solve[d][:, 2], solve[d][:, 0], lf[d].unsqueeze(1).to_broadcast([P, H, P]), ALU.mult).then_inc(pool_step, 1)
                    pool.wait_ge(pool_step, pool_steps())
                    V.tensor_tensor(solve[d][:, 2], id4, solve[d][:, 2], ALU.subtract).then_inc(pool_step, 1)
                    pool.wait_ge(pool_step, pool_steps())
                    pool.sem_inc(inverse_begun, 1)
                    pool.wait_ge(*banks.read_out(("lt", t, d)))
                    V.tensor_tensor(solve[d][:, 3], solve[d][:, 1], lf[1 - d].unsqueeze(1).to_broadcast([P, H, P]), ALU.mult).then_inc(pool_step, 1)
                    pool.wait_ge(pool_step, pool_steps())
                    V.tensor_tensor(solve[d][:, 3], id4, solve[d][:, 3], ALU.subtract).then_inc(pool_step, 1)
                    pool.wait_ge(pool_step, pool_steps())
                    pool.sem_inc(inverse_begun, 1)
                for d in range(2):
                    k4 = kv_tm[:, t, 0:GW].rearrange("p (h n) -> p h n", h=H)
                    v4 = kv_tm[:, t, GW:2 * GW].rearrange("p (h n) -> p h n", h=H)
                    if G(t, d):
                        pool.wait_ge(*banks.full(("uw", *GROUPS[G(t, d) - 1])))
                    else:
                        pool.wait_ge(*banks.read_out("q_tm"))
                    V.tensor_tensor(vk[:, 0], v4, beta[:, t, d, :].unsqueeze(2).to_broadcast([P, H, HD]), ALU.mult).then_inc(pool_step, 1)
                    pool.wait_ge(pool_step, pool_steps())
                    V.tensor_tensor(vk[:, 1], k4, begc[:, d, t, :].unsqueeze(2).to_broadcast([P, H, HD]), ALU.mult).then_inc(pool_step, 1)
                    pool.wait_ge(pool_step, pool_steps())
                    pool.sem_inc(vk_ready, 1)
                    pool.wait_ge(gls_ready, G(t, d) + 1)
                    V.tensor_tensor(kd[:, d, t], k4, ekd[:, d, t, :].unsqueeze(2).to_broadcast([P, H, HD]), ALU.mult).then_inc(pool_step, 1)
                    pool.wait_ge(pool_step, pool_steps())
                    pool.sem_inc(kd_ready, 1)
            pool.wait_ge(head_squares, 1)
            rsqrt(stat[:, 32:48], stat[:, 8:24], 16, 1.0 / HD, EPS)
            pool.sem_inc(head_rstd, 1)
            pool.wait_ge(squares_ready, 2)
            rsqrt(rstat[:, 2:4], rstat[:, 0:2], 2, 1.0 / D, EPS)
            pool.sem_inc(rstd_ready, 1)
            pool.wait_ge(squares_ready, 3)
            rsqrt(rstat[:, 12:14], rstat[:, 10:12], 2, 1.0 / D, EPS)
            pool.sem_inc(rstd_ready, 1)
            pool.wait_ge(squares_ready, 4)
            rsqrt(stat2[:, 2:4], stat2[:, 0:2], 2, 1.0 / D, EPS)
            pool.sem_inc(rstd_ready, 1)
            pool.wait_ge(squares_ready, 5)
            rsqrt(stat2[:, 6:8], stat2[:, 4:6], 2, 1.0 / KVR, EPS)
            pool.sem_inc(rstd_ready, 1)
            pool.wait_ge(chosen_ready, 1)
            pool.wait_ge(*banks.read_out("ckvT"))
            for h in range(AH):
                if h >= 2:
                    pool.wait_ge(hbias_used, h - 1)
                V.tensor_scalar(hbias[h % 2], K2("neg_dist"), SLOPES[h], None, ALU.mult).then_inc(pool_step, 1)
                pool.wait_ge(pool_step, pool_steps())
                V.tensor_tensor(hbias[h % 2], hbias[h % 2], chosen, ALU.add).then_inc(pool_step, 1)
                pool.wait_ge(pool_step, pool_steps())
                pool.sem_inc(hbias_ready, 1)
            pool.wait_ge(squares_ready, 6)
            rsqrt(rs2[:, 2:4], rs2[:, 0:2], 2, 1.0 / D, EPS)
            pool.sem_inc(rstd_ready, 1)
            pool.wait_ge(squares_ready, 7)
            rsqrt(rs2[:, 22:24], rs2[:, 20:22], 2, 1.0 / D, EPS)
            pool.sem_inc(rstd_ready, 1)



def chunks_by_column(w, n=256):
    k, c = w.shape
    return np.ascontiguousarray(w.reshape(k // P, P, c // n, n).transpose(2, 1, 0, 3)).reshape(c // n, P, -1)


def lay_out(v):
    f = lambda n: np.asarray(v[n])
    fm = lambda a: np.ascontiguousarray(np.asarray(a).reshape(-1, P).T)
    rep = lambda a: np.broadcast_to(np.asarray(a).reshape(1, -1), (P, np.asarray(a).size))
    a = {}
    a["x"], a["ctx"] = f("x").reshape(NT, P, D), f("ctx").reshape(NT, P, D)
    a["const1"], a["const2"] = const_arrays()
    taps = lambda w, n: np.ascontiguousarray(w.T.reshape(n, P, -1).transpose(1, 0, 2)).reshape(P, -1)
    small = dict(norm1=fm(f("norm1_g")), norm1_2=fm(f("norm1_g_2")), c=fm(f("c")), c_ctx=fm(f("c_ctx")), c_2=fm(f("c_2")),
                 conv=taps(f("dn_conv_w")[0], 6), a_log=rep(f("dn_a_log")), dt_bias=rep(f("dn_dt_bias")),
                 dn_norm=rep(f("dn_norm_g")), df_norm=rep(f("df_norm_g")), df_lambda=rep(f("df_lambda")),
                 router_b=np.concatenate([rep(f("b_group_2")), rep(f("b_expert_2"))], axis=1),
                 conv_2=taps(f("conv_w_2")[0], RT), conv_b_2=fm(f("conv_b_2")), rg_a=fm(f("b_rg_a_2")),
                 rg_x=fm(f("b_rg_x_2")), lru=fm(f("lru_lambda_2")), kv_norm=rep(f("kv_norm_g_2")))
    a["small"] = np.ascontiguousarray(np.concatenate([small[n] for n in SMALL.at], axis=1))
    a["b_mod"] = np.stack([f("b_mod").reshape(24, 256), f("b_mod_2").reshape(24, 256)])
    a["w_mod"], a["w_mod_2"] = chunks_by_column(f("w_mod")[0]), chunks_by_column(f("w_mod_2")[0])
    w = f("w_in")[0]
    a["w_in"] = chunks_by_column(np.concatenate([w[:, c:c + 256] for c in W_IN.values()], axis=1))
    a["w_ab"] = chunks_by_column(w[:, W_IN_AB:W_IN_AB + 16], 16)[0]
    a["w_out"] = chunks_by_column(f("w_out")[0])
    a["ft_w"] = np.ascontiguousarray(f("ft_w")[0].reshape(2, P, GW).transpose(1, 0, 2)).reshape(P, -1)
    q = np.arange(S)
    dy = q[None, :] // GRID - q[:, None] // GRID + 7
    dx = np.clip(q[None, :] % GRID - q[:, None] % GRID, -15, 15) + 15
    a["na_bias"] = np.ascontiguousarray(f("na_rpb")[0][:, dy, dx].reshape(H, NT, P, S).transpose(2, 0, 1, 3)).reshape(P, -1)
    a["norm2_g"], a["final_norm_g"] = f("norm2_g"), f("final_norm_g").reshape(1, D)
    a["w_router"] = chunks_by_column(f("w_router")[0], E1)[0]
    a["w_gate"], a["w_up"] = (f(n).reshape(E1 * KT, P, F1) for n in ("w_gate", "w_up"))
    a["w_down"] = np.ascontiguousarray(f("w_down").reshape(E1 * 8, 2, P, D).transpose(0, 2, 1, 3)).reshape(E1 * 8, P, 2 * D)
    w = f("w_in_2")[0]
    a["w_in_2"] = chunks_by_column(np.concatenate([w[:, c:c + 256] for c in IN2], axis=1))
    ki, wi = w[:, IN2_KI:IN2_KI + IDD], w[:, IN2_WI:IN2_WI + IH]
    a["w_ki"] = chunks_by_column(np.concatenate([ki, ki, wi], axis=1), 2 * IDD + IH)
    kv = lambda n: np.ascontiguousarray(f(n).reshape(2, P, AH * AD).transpose(1, 0, 2)).reshape(1, P, -1)
    a["w_uk"], a["w_uv"] = kv("w_uk_2"), kv("w_uv_2")
    rg = np.stack([f("w_rg_a_2")[0], f("w_rg_x_2")[0]], axis=1)
    a["w_rg"] = np.ascontiguousarray(rg.reshape(2, RT // 2, 2, P, P).transpose(0, 3, 1, 2, 4)).reshape(2, P, -1)
    a["w_rnn_out"] = chunks_by_column(f("w_rnn_out_2")[0], P)
    a["w_att_out"], a["w_out_2"] = chunks_by_column(f("w_att_out_2")[0]), chunks_by_column(f("w_out_2")[0])
    a["w_router_2"] = chunks_by_column(np.concatenate([f("w_group_2")[0], f("w_expert_2")[0]], axis=1), NG2 + E2)[0]
    a["norm2_g_2"], a["final_g_2"] = f("norm2_g_2"), f("final_g_2").reshape(1, D)
    for n in ("1", "3"):
        w = f(f"moe_w{n}_2").reshape(E2, 2, 4, P, F2)
        a["moe_w" + n] = np.ascontiguousarray(w.transpose(0, 1, 3, 2, 4)).reshape(E2 * 2, P, 4 * F2)
    w = f("moe_w2_2").reshape(E2, 2, 2, P, D)
    a["moe_w2"] = np.ascontiguousarray(w.transpose(0, 1, 3, 2, 4)).reshape(E2 * 2, P, 2 * D)
    return a


def kernel(**inputs):
    import concourse.bacc as _bacc
    from concourse.bass_utils import run_bass_kernel_spmd as _run

    nc = _bacc.Bacc("TRN2", target_bir_lowering=False, num_devices=1)
    arrays, args = {}, {}
    for name, a in lay_out(inputs).items():
        arrays["in_" + name] = a
        args[name] = nc.dram_tensor("in_" + name, a.shape, mybir.dt.from_np(a.dtype), kind="ExternalInput").ap()
    out = nc.dram_tensor("out_0", (1, S, D), F32, kind="ExternalOutput").ap()
    build(nc, args, out)
    r = _run(nc, [arrays], core_ids=[0])
    return r.results[0]["out_0"]
```
